# Optimizing a Trainium2 kernel written in Bass

```python
import jax, jax.numpy as jnp
from jax import lax
import numpy as np

D_MODEL = 2048
BATCH = 1
SEQ = 256
DEPTH = 1

MLSTM_HEADS = 8
MLSTM_QK_DIM = D_MODEL // 16
MLSTM_V_DIM = D_MODEL // 8
MLSTM_QK_WIDTH = MLSTM_HEADS * MLSTM_QK_DIM
MLSTM_WIDTH = MLSTM_HEADS * MLSTM_V_DIM
CHUNK = 128
CONV_WIDTH = D_MODEL
CONV_K = 3
D_FF = ((8 * D_MODEL // 3 + 255) // 256) * 256
EPS = 1e-6

IN_SIZES = (MLSTM_QK_WIDTH, MLSTM_QK_WIDTH, MLSTM_WIDTH, MLSTM_WIDTH,
            MLSTM_HEADS, MLSTM_HEADS,
            CONV_WIDTH, CONV_WIDTH, CONV_WIDTH,
            D_MODEL, D_MODEL)
IN_WIDTH = sum(IN_SIZES)

kernel_name = "hybrid_mlstm_shortconv_gated_block"

def rmsnorm(x, g):
    xf = x.astype(jnp.float32)
    r = lax.rsqrt(jnp.mean(xf * xf, axis=-1, keepdims=True) + EPS)
    return (xf * r * g.astype(jnp.float32)).astype(x.dtype)

def split_columns(p):
    idx = []
    acc = 0
    for s in IN_SIZES[:-1]:
        acc += s
        idx.append(acc)
    return jnp.split(p, idx, axis=-1)

def mlstm_chunkwise(q, k, v, i_pre, f_pre):
    bsz, s_len, h, dk = q.shape
    dv = v.shape[-1]
    nc = s_len // CHUNK
    f32 = jnp.float32

    def to_chunks(t):
        return t.astype(f32).reshape(bsz, nc, CHUNK, h, -1).transpose(1, 0, 3, 2, 4)

    def gate_chunks(t):
        return t.astype(f32).reshape(bsz, nc, CHUNK, h).transpose(1, 0, 3, 2)

    log_f = jax.nn.log_sigmoid(f_pre.astype(f32))
    xs = (to_chunks(q), to_chunks(k), to_chunks(v), gate_chunks(i_pre), gate_chunks(log_f))
    causal = jnp.tril(jnp.ones((CHUNK, CHUNK), dtype=bool))

    def step(carry, inp):
        c_state, n_state, m_state = carry
        qc, kc, vc, li, lf = inp
        b = jnp.cumsum(lf, axis=-1)
        g = b[..., -1]
        dmat = b[..., :, None] - b[..., None, :] + li[..., None, :]
        dmat = jnp.where(causal, dmat, -jnp.inf)
        m_inter = b + m_state[..., None]
        m_comb = jnp.maximum(m_inter, jnp.max(dmat, axis=-1))
        w = jnp.exp(dmat - m_comb[..., None])
        scores = jnp.einsum('bhtk,bhsk->bhts', qc, kc) * w
        inter = jnp.exp(m_inter - m_comb)
        num = (jnp.einsum('bhts,bhsv->bhtv', scores, vc)
               + inter[..., None] * jnp.einsum('bhtk,bhkv->bhtv', qc, c_state))
        den = jnp.sum(scores, axis=-1) + inter * jnp.einsum('bhtk,bhk->bht', qc, n_state)
        h_out = num / jnp.maximum(jnp.abs(den), jnp.exp(-m_comb))[..., None]
        a = g[..., None] - b + li
        m_new = jnp.maximum(g + m_state, jnp.max(a, axis=-1))
        decay = jnp.exp(g + m_state - m_new)
        wk = jnp.exp(a - m_new[..., None])
        c_new = decay[..., None, None] * c_state + jnp.einsum('bhs,bhsk,bhsv->bhkv', wk, kc, vc)
        n_new = decay[..., None] * n_state + jnp.einsum('bhs,bhsk->bhk', wk, kc)
        return (c_new, n_new, m_new), h_out

    init = (jnp.zeros((bsz, h, dk, dv), f32), jnp.zeros((bsz, h, dk), f32), jnp.zeros((bsz, h), f32))
    _, hs = lax.scan(step, init, xs)
    return hs.transpose(1, 0, 3, 2, 4).reshape(bsz, s_len, h, dv)

def causal_depthwise_conv(u, w):
    s_len = u.shape[1]
    up = jnp.pad(u, ((0, 0), (CONV_K - 1, 0), (0, 0)))
    y = w[0] * up[:, 0:s_len]
    for j in range(1, CONV_K):
        y = y + w[j] * up[:, j:j + s_len]
    return y

def setup_inputs(seed: int = 0) -> dict:
    key = jax.random.key(seed)
    ks = jax.random.split(key, 16)
    f32 = jnp.float32
    nrm = lambda k, shape, scale: (jax.random.normal(k, shape, f32) * scale).astype(f32)
    x = jax.random.normal(ks[0], (BATCH, SEQ, D_MODEL), f32)
    norm_mix = 1.0 + nrm(ks[1], (DEPTH, D_MODEL), 0.02)
    w_in = nrm(ks[2], (DEPTH, D_MODEL, IN_WIDTH), D_MODEL ** -0.5)
    b_igate = nrm(ks[3], (DEPTH, MLSTM_HEADS), 0.1)
    b_fgate = (jnp.linspace(3.0, 6.0, MLSTM_HEADS, dtype=f32)[None, :]
               + nrm(ks[4], (DEPTH, MLSTM_HEADS), 0.1))
    conv_w = nrm(ks[5], (DEPTH, CONV_K, CONV_WIDTH), CONV_K ** -0.5)
    mh_norm = 1.0 + nrm(ks[6], (DEPTH, MLSTM_WIDTH), 0.02)
    w_branch_a = nrm(ks[7], (DEPTH, MLSTM_WIDTH, D_MODEL), MLSTM_WIDTH ** -0.5)
    w_branch_b = nrm(ks[8], (DEPTH, CONV_WIDTH, D_MODEL), CONV_WIDTH ** -0.5)
    w_out = nrm(ks[9], (DEPTH, D_MODEL, D_MODEL), D_MODEL ** -0.5)
    norm_ffn = 1.0 + nrm(ks[10], (DEPTH, D_MODEL), 0.02)
    w_gate = nrm(ks[11], (DEPTH, D_MODEL, D_FF), D_MODEL ** -0.5)
    w_up = nrm(ks[12], (DEPTH, D_MODEL, D_FF), D_MODEL ** -0.5)
    w_down = nrm(ks[13], (DEPTH, D_FF, D_MODEL), D_FF ** -0.5)
    norm_final = 1.0 + nrm(ks[14], (D_MODEL,), 0.02)
    return {"x": x, "norm_mix": norm_mix, "w_in": w_in, "b_igate": b_igate, "b_fgate": b_fgate,
            "conv_w": conv_w, "mh_norm": mh_norm, "w_branch_a": w_branch_a,
            "w_branch_b": w_branch_b, "w_out": w_out, "norm_ffn": norm_ffn,
            "w_gate": w_gate, "w_up": w_up, "w_down": w_down, "norm_final": norm_final}

def reference(x, norm_mix, w_in, b_igate, b_fgate, conv_w, mh_norm, w_branch_a,
              w_branch_b, w_out, norm_ffn, w_gate, w_up, w_down, norm_final):
    bsz, s_len, _ = x.shape
    for l in range(DEPTH):
        h = rmsnorm(x, norm_mix[l])
        proj = jnp.einsum('bsd,de->bse', h, w_in[l])
        q, k, v, o_pre, i_pre, f_pre, cb, cc, cx, ga, gb = split_columns(proj)

        q = q.reshape(bsz, s_len, MLSTM_HEADS, MLSTM_QK_DIM) * (MLSTM_QK_DIM ** -0.5)
        k = k.reshape(bsz, s_len, MLSTM_HEADS, MLSTM_QK_DIM)
        v = v.reshape(bsz, s_len, MLSTM_HEADS, MLSTM_V_DIM)
        hm = mlstm_chunkwise(q, k, v, i_pre + b_igate[l], f_pre + b_fgate[l])
        hm = hm * lax.rsqrt(jnp.mean(hm * hm, axis=-1, keepdims=True) + EPS)
        hm = hm.reshape(bsz, s_len, MLSTM_WIDTH) * mh_norm[l].astype(jnp.float32)
        hm = (jax.nn.sigmoid(o_pre.astype(jnp.float32)) * hm).astype(x.dtype)
        y_a = jnp.einsum('bse,ed->bsd', hm, w_branch_a[l])

        u = causal_depthwise_conv(cc * cx, conv_w[l])
        y_b = jnp.einsum('bse,ed->bsd', cb * u, w_branch_b[l])

        merged = jax.nn.sigmoid(ga) * y_a + jax.nn.sigmoid(gb) * y_b
        x = x + jnp.einsum('bsd,de->bse', merged, w_out[l])

        hf = rmsnorm(x, norm_ffn[l])
        act = jax.nn.silu(jnp.einsum('bsd,df->bsf', hf, w_gate[l])) * jnp.einsum('bsd,df->bsf', hf, w_up[l])
        x = x + jnp.einsum('bsf,fd->bsd', act, w_down[l])
    return rmsnorm(x, norm_final)


_drawn_inputs = setup_inputs


def setup_inputs(seed=0):
    import zlib

    import numpy as np

    out = dict(_drawn_inputs(seed))
    spreads = {}
    factors = {'b_igate': 64.0, 'mh_norm': 8.0, 'norm_ffn': 4.4, 'norm_final': 7.775}
    for name, (base, spread) in spreads.items():
        noise = np.random.default_rng([zlib.crc32(name.encode()), seed]).standard_normal(out[name].shape)
        drawn = base * np.exp(spread * noise) if base else spread * noise
        out[name] = __import__('jax').numpy.asarray(drawn.astype(out[name].dtype))
    for name, factor in factors.items():
        out[name] = (out[name] * factor).astype(out[name].dtype)
    return out
```

```python
from contextlib import ExitStack

import numpy as np

import concourse.bass as bass
from concourse import mybir

ALU = mybir.AluOpType
ACT = mybir.ActivationFunctionType
AX = mybir.AxisListType
F32 = mybir.dt.float32
F32R = mybir.dt.float32r

P = 128
COLS = 512
RAW_SLOTS = 4
SPLIT_SLOTS = 2
KB = 4
MASKED = -1e30


def starts(turn):
    return isinstance(turn, int) and turn == 0


class Chunk:

    def __init__(self, at, turn=0, stride=0):
        self.at, self.turn, self.stride = at, turn, stride

    def count(self, more):
        return self.at + more + self.turn * self.stride

    def landed(self):
        return 16 * (self.at // RAW_SLOTS + 1) + self.turn * (16 * self.stride // RAW_SLOTS)

    def next(self):
        return Chunk(self.at + 1, self.turn, self.stride)

    @property
    def raw(self):
        return self.at % RAW_SLOTS

    @property
    def split(self):
        return self.at % SPLIT_SLOTS


def hybrid_block(nc, x, norm_mix, w_in, b_igate, b_fgate, conv_w, mh_norm, w_branch_a, w_branch_b,
                 w_out, norm_ffn, w_gate, w_up, w_down, norm_final, out):
    _, SEQ, D = x.shape
    H = b_igate.shape[1]
    DK, DV = D // 16, D // 8
    CHUNK = 128
    RT = SEQ // P
    KC = D // P
    F = w_gate.shape[2]
    FC = F // P
    NB = D // COLS
    FB = F // COLS
    TAPS = conv_w.shape[1]
    EPS = 1e-6
    QK_SCALE = float(DK) ** -0.5
    assert RT == 2 and CHUNK == P and DK == P and KC == 16 and NB == 4 and TAPS == 3

    C_QK, C_V, C_O = 0, 2 * H * DK, 2 * H * DK + H * DV
    C_GATES = C_O + H * DV
    C_CB = C_GATES + 2 * H
    C_CC, C_CX = C_CB + D, C_CB + 2 * D
    C_GA, C_GB = C_CB + 3 * D, C_CB + 4 * D

    BC = KC // KB
    G_QK = 0
    G_V = G_QK + 4 * BC
    G_CONV = G_V + 4 * BC
    G_O = G_CONV + 3 * NB * BC
    G_MERGE = G_O + NB * BC
    G_OUT = G_MERGE + 4 * NB * BC
    G_FFN = G_OUT + NB * BC
    G_DOWN = G_FFN + 2 * FB * BC
    G_END = G_DOWN + FC

    A_V, A_CONV = 4, 8
    A_O = A_CONV + 2 * NB
    A_MERGE = A_O + NB
    A_FFN = A_MERGE + 2 * NB
    V_MERGE = NB
    V_OUT = V_MERGE + 2 * NB
    V_FFN = V_OUT + NB

    flat = lambda w: w.rearrange("o k n -> (o k) n")
    by_k = lambda w: flat(w).rearrange("(k p) n -> p k n", p=P)
    x_rows = x.rearrange("b (r p) d -> p (b r) d", p=P)
    out_rows = out.rearrange("b (r p) d -> p (b r) d", p=P)
    w_in_k, w_a_k, w_b_k, w_out_k = by_k(w_in), by_k(w_branch_a), by_k(w_branch_b), by_k(w_out)
    w_gate_k, w_up_k, w_down_k = by_k(w_gate), by_k(w_up), by_k(w_down)

    with ExitStack() as ctx:
        BASE = -(-nc.sbuf_base // 64) * 64
        CH = KB * COLS * 4
        AT = KC * SEQ * 4
        RING = BASE
        R1 = RING + (RAW_SLOTS + 2 * SPLIT_SLOTS) * CH
        R2 = R1 + 2 * AT
        R3 = R2 + 2 * AT
        Z = R3 + 2 * AT

        def at(name, shape, dt, offset):
            return nc.alloc_sbuf_tensor_at(name, shape, dt, offset=offset)

        w_raw = at("w_raw", [P, RAW_SLOTS, CH // 4], F32, RING)
        w_hi = at("w_hi", [P, SPLIT_SLOTS, CH // 4], F32R, RING + RAW_SLOTS * CH)
        w_lo = at("w_lo", [P, SPLIT_SLOTS, CH // 4], F32R, RING + (RAW_SLOTS + SPLIT_SLOTS) * CH)

        xT_hi, xT_lo = at("xT_hi", [P, KC, SEQ], F32R, R1), at("xT_lo", [P, KC, SEQ], F32R, R1 + AT)
        cuT_hi, cuT_lo = at("cuT_hi", [P, KC, SEQ], F32R, R2), at("cuT_lo", [P, KC, SEQ], F32R, R2 + AT)
        hmT_hi, hmT_lo = at("hmT_hi", [P, KC, SEQ], F32R, R3), at("hmT_lo", [P, KC, SEQ], F32R, R3 + AT)
        xn = at("xn", [P, RT, D], F32, R2)
        GH = KC * P * 4
        wg_hi, wg_lo = at("wg_hi", [P, KC, P], F32R, R2 + AT), at("wg_lo", [P, KC, P], F32R, R2 + AT + GH)
        qk = at("qk", [P, RT, 2 * H * DK], F32, R3)
        s = R3 + RT * 2 * H * DK * 4
        head_qk = at("head_qk", [P, 2, 4, P], F32, s)
        head_qkT = at("head_qkT", [P, 2, 4, P], F32, s + 4096)
        head_w = at("head_w", [P, 2, RT, P], F32, s + 8192)
        head_sc = at("head_sc", [P, 2, RT, P], F32, s + 10240)
        head_kw = at("head_kw", [P, 2, P], F32, s + 12288)
        head_C = at("head_C", [P, 2, DV + 1], F32, s + 13312)
        actT = at("actT", [P, FC, SEQ], F32, R1)
        x1 = at("x1", [P, RT, D], F32, R2 + AT)
        assert R1 + FC * SEQ * 4 <= R2 + AT
        fT_hi, fT_lo = at("fT_hi", [P, KC, SEQ], F32R, R3), at("fT_lo", [P, KC, SEQ], F32R, R3 + AT)

        VX = RT * H * (DV + 1) * 4
        vx = at("vx", [P, RT, H, DV + 1], F32, Z)
        sq_x = at("sq_x", [P, D], F32, Z)
        vec_rows = at("vec_rows", [96, P], F32, Z + 8192)
        wg_raw = at("wg_raw", [P, KC, 2 * H], F32, Z + 8192 + 512)
        s = Z + VX
        nat = at("nat", [P, RT, COLS], F32, s)
        pT = at("pT", [P, KB, SEQ + 32], F32, s + 4096)
        PAD = 32 - (TAPS - 1)
        s += 4096 + KB * (SEQ + 32) * 4
        uT = at("uT", [P, KB, SEQ], F32, s)
        cbT = at("cbT", [P, KB, SEQ], F32, s + 4096)
        hm = at("hm", [P, RT, COLS], F32, s + 4096)
        s += 8192
        row = lambda name, k, n=RT: at(name, [H, n, P], F32, s + 1024 * k)
        r_a, r_lf, r_t, r_b, r_M, r_bM, r_negM = (row(n, k) for k, n in enumerate(
            ["r_a", "r_lf", "r_t", "r_b", "r_M", "r_bM", "r_negM"]))
        r_emc, r_wk, r_int = row("r_emc", 7), row("r_wk", 8, 1), at("r_int", [H, 1, P], F32, s + 8704)
        sel = [row("sel0", 0), row("sel1", 1)]
        s += 9216
        inter = at("inter", [P, DV + 1], F32, s)
        num = at("num", [P, DV + 1], F32, s + 1056)
        mT_hi, mT_lo = at("mT_hi", [P, KC, SEQ], F32R, Z), at("mT_lo", [P, KC, SEQ], F32R, Z + AT)
        gate = at("gate", [P, RT, COLS], F32, Z + 2 * AT)
        prod = at("prod", [P, RT, COLS], F32, Z + 2 * AT + 4096)
        merged = at("merged", [P, RT, COLS], F32, Z + 2 * AT + 8192)
        g_final = at("g_final", [P, D], F32, Z)
        y = at("y", [P, RT, D], F32, Z + D * 4)
        sq_y = at("sq_y", [P, D], F32, Z + 3 * D * 4)
        CONST = Z + 2 * AT + 12288
        assert s + 2 * 1056 <= CONST, (s, CONST)
        s = CONST
        ident = at("ident", [P, P], F32, s)
        causal = at("causal", [P, P], F32, s + 512)
        vecT = at("vecT", [P, 96], F32, s + 1024)
        ones = at("ones", [H, P], F32, s + 1408)
        cols = at("cols", [P, 6, H], F32, s + 1920)
        head_cols = at("head_cols", [P, 2, 6], F32, s + 2112)
        gate_bias = at("gate_bias", [P, 1], F32, s + 2176)
        half = at("half", [P, 2 * H], F32, s + 2208)
        ss = at("ss", [P, 2 * H], F32, s + 2272)
        rstd = at("rstd", [P, 2 * H], F32, s + 2336)
        ss1 = at("ss1", [P, RT, NB], F32, s + 2400)
        ssx = at("ssx", [P, 2, RT], F32, s + 2432)
        r_x = at("r_x", [P, 2, RT], F32, s + 2464)
        den = at("den", [P, 4], F32, s + 2496)
        sums = at("sums", [P, RT], F32, s + 2528)
        a_hi = at("a_hi", [P, 2, SEQ], F32R, CONST - 8192)
        a_lo = at("a_lo", [P, 2, SEQ], F32R, CONST - 8192 + 2048)
        sq_h = at("sq_h", [P, DV], F32, CONST - 8192)
        assert s + 2560 <= nc.sbuf_usable_end, (s + 2560, nc.sbuf_usable_end)
        A_IN, WK, INT, EMC = 0, 2, 3, 4
        V_MIX, V_MH, V_FN, V_TAP = 0, KC, 2 * KC, 3 * KC

        ps = ctx.enter_context(nc.psum_tensor("ps", [P, 8, COLS], F32))

        def sem(name):
            return ctx.enter_context(nc.semaphore(name))

        raw_landed = [sem(f"raw_landed{n}") for n in range(RAW_SLOTS)]
        hi_split, lo_split = sem("hi_split"), sem("lo_split")
        hi_used, lo_used = sem("hi_used"), sem("lo_used")
        act_out, dve_out = sem("act_out"), sem("dve_out")
        x_landed = [sem(f"x_landed{n}") for n in range(RT)]
        small_landed = [sem(f"small_landed{n}") for n in range(4)]
        x_again, final_landed, stored = sem("x_again"), sem("final_landed"), [sem("stored0"), sem("stored1")]
        setup, setup2 = sem("setup"), sem("setup2")
        x_squared, x_mean, x_rstd, x_normed = sem("x_squared"), sem("x_mean"), sem("x_rstd"), sem("x_normed")
        vec_turned, vec_ready = sem("vec_turned"), sem("vec_ready")
        x_turned, x_hi_done, x_lo_done = sem("x_turned"), sem("x_hi_done"), sem("x_lo_done")
        gw_hi, gw_lo, gates_done = sem("gw_hi"), sem("gw_lo"), sem("gates_done")
        rows_dve, rows_act, cols_turned, cols_ready = sem("rows_dve"), sem("rows_act"), sem("cols_turned"), sem("cols_ready")
        staged, turned, turned_out = sem("staged"), sem("turned"), sem("turned_out")
        selected, scored, weighed, exped, scores_done = (sem("selected"), sem("scored"), sem("weighed"),
                                                         sem("exped"), sem("scores_done"))
        kw_done, first_done, state_out, h0_done = sem("kw_done"), sem("first_done"), sem("state_out"), sem("h0_done")
        second_done, inter_out, h1_done, den_step = sem("second_done"), sem("inter_out"), sem("h1_done"), sem("den_step")
        cb_turned, cb_out = sem("cb_turned"), sem("cb_out")
        p_turned, p_copied, p_read = sem("p_turned"), sem("p_copied"), sem("p_read")
        tap_step, u_done, cu_hi, cu_lo = sem("tap_step"), sem("u_done"), sem("cu_hi"), sem("cu_lo")
        h_squared, h_mean, h_rstd, hm_done = sem("h_squared"), sem("h_mean"), sem("h_rstd"), sem("hm_done")
        grp_turned, grp_hi, grp_lo = sem("grp_turned"), sem("grp_hi"), sem("grp_lo")
        m_done, x1_squared, x1_summed, x1_mean, x1_rstd = (sem("m_done"), sem("x1_squared"), sem("x1_summed"),
                                                           sem("x1_mean"), sem("x1_rstd"))
        act_turned, act_out_of = sem("act_turned"), sem("act_out_of")
        a_hi_staged, a_lo_staged = sem("a_hi_staged"), sem("a_lo_staged")
        down_done, y_sum, y_squared, y_mean, y_rstd, y_done = (sem("down_done"), sem("y_sum"), sem("y_squared"),
                                                               sem("y_mean"), sem("y_rstd"), sem("y_done"))

        block = ctx.enter_context(nc.Block())

        GRP_HM, GRP_M, GRP_F = 0, NB, 2 * NB
        HI_HM, HI_M, HI_F = 0, NB * KB, NB * KB + NB

        @block.sync
        def _(sp):
            def load(chunk, source):
                if not (isinstance(chunk.turn, int) and chunk.count(0) < RAW_SLOTS):
                    sp.wait_ge(lo_split, chunk.count(1 - RAW_SLOTS))
                dst = w_raw[:, chunk.raw, :]
                if len(source.shape) == 3:
                    dst = dst.rearrange("p (k n) -> p k n", k=KB)
                sp.dma_start(dst, source).then_inc(raw_landed[chunk.raw], 16)

            def load_block(at_chunk, turn, stride, w, col):
                for q in range(BC):
                    load(Chunk(at_chunk + q, turn, stride), w[:, q * KB:(q + 1) * KB, bass.ds(col, COLS)])

            kp = lambda v: v.rearrange("o (k p) -> (o k) p", p=P)
            sp.dma_start(xn[:, 0, :], x_rows[:, 0, :]).then_inc(x_landed[0], 16)
            sp.dma_start(xn[:, 1, :], x_rows[:, 1, :]).then_inc(x_landed[1], 16)
            sp.dma_start(vec_rows[V_MIX:V_MIX + KC, :], kp(norm_mix)).then_inc(small_landed[0], 16)
            sp.dma_start(vec_rows[V_MH:V_MH + KC, :], kp(mh_norm)).then_inc(small_landed[0], 16)
            sp.dma_start(vec_rows[V_FN:V_FN + KC, :], kp(norm_ffn)).then_inc(small_landed[0], 16)
            sp.dma_start(vec_rows[V_TAP:V_TAP + TAPS * KC, :],
                         conv_w.rearrange("o j (k p) -> (o j k) p", p=P)).then_inc(small_landed[0], 16)
            load_block(G_QK, 0, 0, w_in_k, C_QK)
            sp.dma_start(wg_raw[:], w_in_k[:, :, C_GATES:C_GATES + 2 * H]).then_inc(small_landed[1], 16)
            sp.dma_start(gate_bias[0:H, :], b_igate.rearrange("o h -> h o")).then_inc(small_landed[2], 16)
            sp.dma_start(gate_bias[32:32 + H, :], b_fgate.rearrange("o h -> h o")).then_inc(small_landed[2], 16)
            load_block(G_QK + BC, 0, 0, w_in_k, C_QK + COLS)
            for n in range(2, 4):
                load_block(G_QK + n * BC, 0, 0, w_in_k, C_QK + n * COLS)
            with sp.Fori(0, 4) as i:
                load_block(G_V, i, BC, w_in_k, C_V + i * COLS)
            with sp.Fori(0, NB) as i:
                for n, c in enumerate((C_CB, C_CC, C_CX)):
                    load_block(G_CONV + n * BC, i, 3 * BC, w_in_k, c + i * COLS)
            with sp.Fori(0, NB) as i:
                load_block(G_O, i, BC, w_in_k, C_O + i * COLS)
            with sp.Fori(1, NB + 1) as i:
                for n, (w, c) in enumerate(((w_in_k, C_GA), (w_a_k, 0), (w_in_k, C_GB), (w_b_k, 0))):
                    load_block(G_MERGE + (n - 4) * BC, i, 4 * BC, w, i * COLS + (c - COLS))
            load_block(G_OUT, 0, 0, w_out_k, 0)
            load(Chunk(G_OUT + BC), w_out_k[:, 0:KB, COLS:2 * COLS])
            sp.wait_ge(lo_used, G_OUT)
            sp.dma_start(x1[:], x_rows).then_inc(x_again, 16)
            for q in range(1, BC):
                load(Chunk(G_OUT + BC + q), w_out_k[:, q * KB:(q + 1) * KB, COLS:2 * COLS])
            with sp.Fori(2, NB) as i:
                load_block(G_OUT, i, BC, w_out_k, i * COLS)

            def load_ffn(i):
                load_block(G_FFN, i, 2 * BC, w_gate_k, i * COLS)
                load_block(G_FFN + BC, i, 2 * BC, w_up_k, i * COLS)

            load_ffn(0)
            sp.wait_ge(lo_used, G_FFN)
            sp.dma_start(g_final[:], norm_final.rearrange("(a n) -> a n", a=1).to_broadcast([P, D])).then_inc(
                final_landed, 16)
            with sp.Fori(1, FB) as i:
                load_ffn(i)
            with sp.Fori(0, FC // RAW_SLOTS) as i:
                for n in range(RAW_SLOTS):
                    load(Chunk(G_DOWN + n, i, RAW_SLOTS), w_down_k[:, i * RAW_SLOTS + n, :])
            for r in range(RT):
                sp.wait_ge(y_done, r + 1)
                sp.dma_start(out_rows[:, r, :], y[:, r, :]).then_inc(stored[r], 16)
            for r in range(RT):
                sp.wait_ge(stored[r], 16)

        @block.gpsimd
        def _(pool):
            pool.memset(ident[:], 0.0).then_inc(setup, 1)
            pool.memset(causal[:], 0.0).then_inc(setup, 1)
            pool.wait_ge(setup, 2)
            pool.affine_select(out=ident[:], in_=ident[:], compare_op=ALU.not_equal, fill=1.0, base=0,
                               pattern=[[-1, P]], channel_multiplier=1).then_inc(setup, 1)
            pool.memset(half[:], -0.5).then_inc(setup, 1)
            pool.memset(ones[:], 1.0).then_inc(setup2, 1)
            pool.affine_select(out=causal[:], in_=causal[:], compare_op=ALU.is_ge, fill=MASKED, base=0,
                               pattern=[[1, P]], channel_multiplier=-1).then_inc(setup2, 1)
            pool.memset(wg_hi[:].bitcast(F32), 0.0).then_inc(setup2, 1)
            pool.memset(wg_lo[:].bitcast(F32), 0.0).then_inc(setup2, 1)

            def rstd_of(mean, source, total, result, squared, width, done):
                nc.gpsimd.tensor_scalar(out=total, in0=source, scalar1=1.0 / width, scalar2=EPS,
                                        op0=ALU.mult, op1=ALU.add).then_inc(mean, 1)
                pool.wait_ge(mean, squared)
                nc.gpsimd.tensor_tensor(out=result, in0=total, in1=half[:, 0:result.shape[1]],
                                        op=ALU.pow).then_inc(done, 1)

            pool.wait_ge(setup, 4)
            for r in range(RT):
                pool.wait_ge(x_squared, r + 1)
                rstd_of(x_mean, ssx[:, 0, r:r + 1], ssx[:, 1, r:r + 1], r_x[:, 0, r:r + 1], r + 1, D, x_rstd)
            pool.wait_ge(x_lo_done, KC)
            pool.wait_ge(gw_lo, 1)
            pool.memset(vx[:, :, :, DV:DV + 1], 1.0).then_inc(setup2, 1)
            pool.memset(pT[:, :, PAD:PAD + TAPS - 1], 0.0).then_inc(setup2, 1)

            qk_heads = qk[:].rearrange("p r (g n) -> p g r n", g=2)

            def stage(i):
                for b in range(2):
                    if not starts(i):
                        pool.wait_ge(h1_done, i * 2 + b - 1)
                    nc.gpsimd.tensor_copy(head_qk[:, b, :, :].rearrange("p (g r) n -> p g r n", g=2),
                                          qk_heads[:, :, :, bass.ds((i * 2 + b) * DK, DK)])
                    nc.gpsimd.tensor_copy(head_cols[:, b, :], cols[:, :, i * 2 + b]).then_inc(staged, 1)

            pool.wait_ge(act_out, A_V)
            pool.wait_ge(cols_ready, 1)
            stage(0)
            with pool.Fori(1, NB) as i:
                stage(i)

            pool.wait_ge(h_squared, RT * H)
            rstd_of(h_mean, ss[:], ss[:], rstd[:], 1, DV, h_rstd)
            pool.wait_ge(x1_summed, 1)
            rstd_of(x1_mean, sums[:], sums[:], r_x[:, 1, :], 1, D, x1_rstd)
            for r in range(RT):
                pool.wait_ge(y_squared, r + 1)
                rstd_of(y_mean, ssx[:, 0, r:r + 1], ssx[:, 1, r:r + 1], r_x[:, 0, r:r + 1], r + 1, D, y_rstd)

        @block.scalar
        def _(act):
            copy = lambda o, i, **kw: nc.scalar.activation(o, i, ACT.Copy, **kw)

            def split(chunk):
                act.wait_ge(raw_landed[chunk.raw], chunk.landed())
                if not (isinstance(chunk.turn, int) and chunk.count(0) < SPLIT_SLOTS):
                    act.wait_ge(hi_used, chunk.count(1 - SPLIT_SLOTS))
                    act.wait_ge(lo_split, chunk.count(1 - SPLIT_SLOTS))
                copy(w_hi[:, chunk.split, :], w_raw[:, chunk.raw, :]).then_inc(hi_split, 1)

            def take(chunk, pair, dst, func=ACT.Copy):
                act.wait_ge(lo_used, chunk.count(1))
                nc.scalar.activation(dst, ps[:, 2 * pair:2 * pair + 2, :], func).then_inc(act_out, 1)

            bank_kt = lambda b0: ps[:, b0:b0 + 2, :].rearrange("p b (k t) -> p (b k) t", k=2)

            def group_hi(n, dst, k0, step, scale_at=None):
                act.wait_ge(grp_turned, n)
                src = bank_kt(4)
                if scale_at is None:
                    copy(dst[:, bass.ds(k0, KB), :], src).then_inc(grp_hi, 1)
                    return
                for k in range(KB):
                    c = scale_at + k0 + k
                    copy(dst[:, k0 + k, :], src[:, k, :], scale=vecT[:, c:c + 1]).then_inc(grp_hi, 1)

            for r in range(RT):
                act.wait_ge(x_landed[r], 16)
                if r > 0:
                    act.wait_ge(x_squared, r)
                nc.scalar.activation(sq_x[:], xn[:, r, :], ACT.Square,
                                     accum_out=ssx[:, 0, r:r + 1]).then_inc(x_squared, 1)
                if r == 0:
                    act.wait_ge(vec_turned, 1)
                    copy(vecT[:], ps[:, 0, 0:96]).then_inc(vec_ready, 1)
            split(Chunk(G_QK))
            act.wait_ge(vec_ready, 1)
            for k in range(KC):
                act.wait_ge(x_turned, k // 2 + 1)
                copy(xT_hi[:, k, :], ps[:, 4 + k // 2 % 4, (k % 2) * SEQ:(k % 2 + 1) * SEQ],
                     scale=vecT[:, V_MIX + k:V_MIX + k + 1]).then_inc(x_hi_done, 1)

            def qk_turn(i):
                for n in range(2):
                    for q in range(BC):
                        c = Chunk(G_QK + n * BC + q, i, 2 * BC)
                        split(c.next())
                    take(c, n, qk[:, :, bass.ds((i * 2 + n) * COLS, COLS)])

            for q in range(BC):
                c = Chunk(G_QK + q)
                split(c.next())
                if q == 1:
                    act.wait_ge(small_landed[1], 16)
                    act.wait_ge(setup2, 4)
                    copy(wg_hi[:, :, 0:64].rearrange("p k (g c) -> p k g c", g=2)[:, :, :, 0:H],
                         wg_raw[:].rearrange("p k (g c) -> p k g c", g=2)).then_inc(gw_hi, 1)
            take(c, 0, qk[:, :, 0:COLS])
            for q in range(BC):
                c = Chunk(G_QK + BC + q)
                split(c.next())
            take(c, 1, qk[:, :, COLS:2 * COLS])
            with act.Fori(1, 2) as i:
                qk_turn(i)

            def gate_rows_1():
                act.wait_ge(rows_dve, 3)
                nc.scalar.activation(r_t[:], r_t[:], ACT.Exp).then_inc(rows_act, 1)
                act.wait_ge(rows_act, 1)
                nc.scalar.activation(r_t[:], r_t[:], ACT.Ln, bias=1.0).then_inc(rows_act, 1)

            def gate_rows_2():
                act.wait_ge(rows_dve, 12)
                nc.scalar.activation(r_wk[:, 0, :], r_a[:, 0, :], ACT.Exp, bias=r_negM[:, 0, P - 1:P])
                nc.scalar.activation(r_int[:, 0, :], r_negM[:, 1, :], ACT.Exp, bias=r_bM[:, 0, P - 1:P])
                nc.scalar.activation(r_emc[:], r_bM[:], ACT.Exp, scale=-1.0).then_inc(rows_act, 1)

            def v_turn(i):
                for n in range(2):
                    for q in range(BC):
                        c = Chunk(G_V + n * BC + q, i, 2 * BC)
                        split(c.next())
                        if starts(i) and n == 0 and q == 0:
                            act.wait_ge(setup2, 6)
                            gate_rows_1()
                        if starts(i) and n == 0 and q == 2:
                            gate_rows_2()
                    act.wait_ge(lo_used, c.count(1))
                    heads = vx[:, :, bass.ds(i * 4 + n * 2, 2), 0:DV]
                    copy(heads, ps[:, 2 * n:2 * n + 2, :].rearrange("p r (h d) -> p r h d", h=2)).then_inc(act_out, 1)

            v_turn(0)
            with act.Fori(1, 2) as i:
                v_turn(i)

            def p_taken(d):
                act.wait_ge(p_turned, d + 1)
                if not starts(d):
                    act.wait_ge(cu_lo, d)
                copy(pT[:, :, 32:32 + SEQ], bank_kt(6)).then_inc(p_copied, 1)
                for k in range(KB):
                    last = copy(uT[:, k, :], bank_kt(6)[:, k, :],
                                scale=vecT[:, bass.ds(V_TAP + (TAPS - 1) * KC + k + d * KB, 1)])
                last.then_inc(p_read, 1)

            def cu_high(d):
                act.wait_ge(u_done, d + 1)
                copy(cuT_hi[:, bass.ds(d * KB, KB), :], uT[:]).then_inc(cu_hi, 1)

            def conv_turn(i):
                first = starts(i)

                def state(b):
                    act.wait_ge(first_done, i * 2 + b + 1)
                    copy(head_C[:, b, :], ps[:, 7, 0:DV + 1]).then_inc(state_out, 1)

                def carried(b):
                    act.wait_ge(second_done, i * 2 + b + 1)
                    if not (first and b == 0):
                        act.wait_ge(h1_done, i * 2 + b)
                    copy(inter[:], ps[:, 7, 0:DV + 1], scale=head_cols[:, b, INT:INT + 1]).then_inc(inter_out, 1)

                for j in range(3 * BC):
                    c = Chunk(G_CONV + j, i, 3 * BC)
                    split(c.next())
                    if j == 0 and not first:
                        p_taken(i - 1)
                    if j == 2:
                        if not first:
                            cu_high(i - 1)
                            act.wait_ge(second_done, i * 2)
                        for b in range(2):
                            act.wait_ge(turned, i * 2 + b + 1)
                            copy(head_qkT[:, b, 0:2, :], ps[:, 6 + b, 0:2 * P], scale=QK_SCALE)
                            copy(head_qkT[:, b, 2:4, :], ps[:, 6 + b, 2 * P:4 * P]).then_inc(turned_out, 1)
                    if j == 3:
                        if not first:
                            act.wait_ge(p_turned, i)
                        take(c, 0, nat[:])
                        for b in range(2):
                            act.wait_ge(weighed, i * 2 + b + 1)
                            for r in range(RT):
                                last = nc.scalar.activation(head_w[:, b, r, :], head_w[:, b, r, :], ACT.Exp,
                                                            bias=head_cols[:, b, A_IN + r:A_IN + r + 1])
                            last.then_inc(exped, 1)
                    if j == 5:
                        act.wait_ge(cb_turned, i + 1)
                        if not first:
                            act.wait_ge(u_done, i)
                        copy(cbT[:], bank_kt(6)).then_inc(cb_out, 1)
                    if j == 6:
                        state(0)
                    if j == 7:
                        take(c, 1, nat[:])
                        carried(0)
                    if j == 8:
                        state(1)
                    if j == 9:
                        carried(1)

            conv_turn(0)
            with act.Fori(1, NB) as i:
                conv_turn(i)

            for n in range(NB):
                for q in range(BC):
                    c = Chunk(G_O + n * BC + q)
                    split(c.next())
                    if n == 0:
                        if q == 0:
                            p_taken(NB - 1)
                            act.wait_ge(h1_done, H)
                        if q == 2:
                            cu_high(NB - 1)
                        for k in range(q * 4, q * 4 + 4):
                            if k > 0:
                                act.wait_ge(h_squared, k)
                            nc.scalar.activation(sq_h[:], vx[:, k // H, k % H, 0:DV], ACT.Square,
                                                 accum_out=ss[:, k:k + 1]).then_inc(h_squared, 1)
                    if n > 0 and q == 1:
                        group_hi(GRP_HM + n, hmT_hi, (n - 1) * KB, 0, V_MH)
                if n > 0:
                    act.wait_ge(hm_done, n)
                else:
                    act.wait_ge(p_turned, NB)
                take(c, n % 2, nat[:], ACT.Sigmoid)

            def merge_turn(i):
                first = starts(i)
                for j in range(4 * BC):
                    c = Chunk(G_MERGE + j, i, 4 * BC)
                    split(c.next())
                    if j == 1:
                        if first:
                            group_hi(GRP_M, hmT_hi, (NB - 1) * KB, 0, V_MH)
                        else:
                            group_hi(i + GRP_M, mT_hi, (i - 1) * KB, 0)
                    if j == 3:
                        if not first:
                            act.wait_ge(dve_out, V_MERGE + i * 2)
                        take(c, 0, gate[:], ACT.Sigmoid)
                    if j == 3 + 2 * BC:
                        act.wait_ge(dve_out, V_MERGE + 1 + i * 2)
                        take(c, 0, gate[:], ACT.Sigmoid)

            merge_turn(0)
            with act.Fori(1, NB) as i:
                merge_turn(i)

            for n in range(NB):
                for q in range(BC):
                    c = Chunk(G_OUT + n * BC + q)
                    split(c.next())
                    if q == 1:
                        if n == 0:
                            group_hi(GRP_F, mT_hi, (NB - 1) * KB, 0)
                        else:
                            group_hi(GRP_F + n, fT_hi, (n - 1) * KB, 0, V_FN)
                act.wait_ge(dve_out, V_OUT + n + 1)
                for r in range(RT):
                    if n + r > 0:
                        act.wait_ge(x1_squared, n * RT + r)
                    nc.scalar.activation(prod[:, 0, :], x1[:, r, n * COLS:(n + 1) * COLS], ACT.Square,
                                         accum_out=ss1[:, r, n:n + 1]).then_inc(x1_squared, 1)

            def act_taken(d):
                act.wait_ge(act_turned, d + 1)
                copy(actT[:, bass.ds(d * KB, KB), :], bank_kt(4)).then_inc(act_out_of, 1)

            def ffn_turn(i):
                first = starts(i)
                for j in range(2 * BC):
                    c = Chunk(G_FFN + j, i, 2 * BC)
                    split(c.next())
                    if j == 1:
                        if first:
                            group_hi(GRP_F + NB, fT_hi, (NB - 1) * KB, 0, V_FN)
                        else:
                            act_taken(i - 1)
                    if j == 3:
                        act.wait_ge(lo_used, c.count(1))
                        if first:
                            act.wait_ge(x1_rstd, 1)
                        else:
                            act.wait_ge(dve_out, V_FFN + i)
                        for r in range(RT):
                            last = nc.scalar.activation(gate[:, r, :], ps[:, r, :], ACT.Silu, scale=r_x[:, 1, r:r + 1])
                        last.then_inc(act_out, 1)

            ffn_turn(0)
            with act.Fori(1, FB) as i:
                ffn_turn(i)
            act_taken(FB - 1)

            def stage(chunk):
                if not (isinstance(chunk.turn, int) and chunk.count(0) < G_DOWN + 2):
                    act.wait_ge(lo_used, chunk.count(-1))
                copy(a_hi[:, chunk.split, :], actT[:, chunk.count(-G_DOWN), :]).then_inc(a_hi_staged, 1)

            stage(Chunk(G_DOWN))

            def down_turn(i, last=False):
                for n in range(RAW_SLOTS):
                    c = Chunk(G_DOWN + n, i, RAW_SLOTS)
                    if not (last and n == RAW_SLOTS - 1):
                        split(c.next())
                        stage(c.next())

            down_turn(0)
            with act.Fori(1, FC // RAW_SLOTS - 1) as i:
                down_turn(i)
            down_turn(FC // RAW_SLOTS - 1, last=True)
            for r in range(RT):
                act.wait_ge(y_sum, r + 1)
                if r > 0:
                    act.wait_ge(y_squared, r)
                nc.scalar.activation(sq_y[:], x1[:, r, :], ACT.Square,
                                     accum_out=ssx[:, 0, r:r + 1]).then_inc(y_squared, 1)

        @block.vector
        def _(dve):
            V = nc.vector

            def split(chunk):
                dve.wait_ge(hi_split, chunk.count(1))
                if not (isinstance(chunk.turn, int) and chunk.count(0) < SPLIT_SLOTS):
                    dve.wait_ge(lo_used, chunk.count(1 - SPLIT_SLOTS))
                V.tensor_tensor(w_lo[:, chunk.split, :], w_raw[:, chunk.raw, :],
                                w_hi[:, chunk.split, :].bitcast(F32), ALU.subtract).then_inc(lo_split, 1)

            bank_kt = lambda b0: ps[:, b0:b0 + 2, :].rearrange("p b (k t) -> p (b k) t", k=2)

            def group_lo(n, steps, dst, hi, k0, scale_at=None):
                src = bank_kt(4)
                if scale_at is None:
                    dve.wait_ge(grp_hi, steps + 1)
                    V.tensor_tensor(dst[:, bass.ds(k0, KB), :], src, hi[:, bass.ds(k0, KB), :].bitcast(F32),
                                    ALU.subtract).then_inc(grp_lo, 1)
                    return
                for k in range(KB):
                    if k % 2 == 0:
                        dve.wait_ge(grp_hi, steps + k + 2)
                    c = scale_at + k0 + k
                    last = V.scalar_tensor_tensor(out=dst[:, k0 + k, :], in0=src[:, k, :], scalar=vecT[:, c:c + 1],
                                                  in1=hi[:, k0 + k, :].bitcast(F32), op0=ALU.mult, op1=ALU.subtract)
                last.then_inc(grp_lo, 1)

            for r in range(RT):
                dve.wait_ge(x_rstd, r + 1)
                V.tensor_scalar(out=xn[:, r, :], in0=xn[:, r, :], scalar1=r_x[:, 0, r:r + 1], scalar2=None,
                                op0=ALU.mult).then_inc(x_normed, 1)
            split(Chunk(G_QK))
            for k in range(KC):
                if k % 2 == 0:
                    dve.wait_ge(x_hi_done, k + 2)
                V.scalar_tensor_tensor(out=xT_lo[:, k, :], in0=ps[:, 4 + k // 2 % 4, (k % 2) * SEQ:(k % 2 + 1) * SEQ],
                                       scalar=vecT[:, V_MIX + k:V_MIX + k + 1], in1=xT_hi[:, k, :].bitcast(F32),
                                       op0=ALU.mult, op1=ALU.subtract).then_inc(x_lo_done, 1)
            for q in range(BC):
                split(Chunk(G_QK + q).next())
                if q == 1:
                    dve.wait_ge(gw_hi, 1)
                    V.tensor_tensor(wg_lo[:, :, 0:64].rearrange("p k (g c) -> p k g c", g=2)[:, :, :, 0:H],
                                    wg_raw[:].rearrange("p k (g c) -> p k g c", g=2),
                                    wg_hi[:, :, 0:64].rearrange("p k (g c) -> p k g c", g=2)[:, :, :, 0:H].bitcast(F32),
                                    ALU.subtract).then_inc(gw_lo, 1)
            with dve.Fori(1, 4) as i:
                for q in range(BC):
                    split(Chunk(G_QK + q, i, BC).next())

            def step(ins, n):
                ins.then_inc(rows_dve, 1)
                dve.wait_ge(rows_dve, n)

            def gate_rows_1():
                dve.wait_ge(gates_done, 1)
                dve.wait_ge(small_landed[2], 32)
                li, f = ps[0:H, 6, 0:SEQ], ps[32:32 + H, 6, 0:SEQ]
                V.tensor_scalar(out=r_a[:], in0=li, scalar1=gate_bias[0:H, :], scalar2=None,
                                op0=ALU.add).then_inc(rows_dve, 1)
                step(V.tensor_scalar(out=r_lf[:], in0=f, scalar1=gate_bias[32:32 + H, :], scalar2=None,
                                     op0=ALU.add), 2)
                V.scalar_tensor_tensor(out=r_t[:], in0=r_lf[:], scalar=-1.0, in1=r_lf[:], op0=ALU.mult,
                                       op1=ALU.min).then_inc(rows_dve, 1)

            def gate_rows_2():
                dve.wait_ge(rows_dve, 3)
                dve.wait_ge(rows_act, 2)
                step(V.scalar_tensor_tensor(out=r_lf[:], in0=r_lf[:], scalar=0.0, in1=r_t[:], op0=ALU.min,
                                            op1=ALU.subtract), 4)
                V.tensor_tensor_scan(r_b[:, 0, :], ones[:], r_lf[:, 0, :], 0.0, ALU.mult, ALU.add).then_inc(rows_dve, 1)
                step(V.tensor_tensor_scan(r_b[:, 1, :], ones[:], r_lf[:, 1, :], 0.0, ALU.mult, ALU.add), 6)
                step(V.tensor_tensor(r_a[:], r_a[:], r_b[:], ALU.subtract), 7)
                step(V.tensor_tensor_scan(r_M[:, 0, :], ones[:], r_a[:, 0, :], 0.0, ALU.mult, ALU.max), 8)
                step(V.tensor_tensor(r_bM[:, 0, :], r_M[:, 0, :], r_b[:, 0, :], ALU.add), 9)
                step(V.tensor_tensor_scan(r_M[:, 1, :], ones[:], r_a[:, 1, :], r_bM[:, 0, P - 1:P], ALU.mult,
                                          ALU.max), 10)
                V.tensor_tensor(r_bM[:, 1, :], r_M[:, 1, :], r_b[:, 1, :], ALU.add).then_inc(rows_dve, 1)
                V.tensor_scalar(out=r_negM[:], in0=r_M[:], scalar1=-1.0, scalar2=None,
                                op0=ALU.mult).then_inc(rows_dve, 1)

            for q in range(BC):
                split(Chunk(G_V + q).next())
                if q == 0:
                    dve.wait_ge(setup2, 6)
                    gate_rows_1()
                if q == 1:
                    gate_rows_2()
            with dve.Fori(1, 4) as i:
                for q in range(BC):
                    split(Chunk(G_V + q, i, BC).next())
            dve.wait_ge(cols_turned, 1)
            V.tensor_copy(cols[:].rearrange("p a h -> p (a h)"), ps[:, 7, 0:6 * H]).then_inc(cols_ready, 1)

            def tap(d, j):
                for k in range(KB):
                    last = V.scalar_tensor_tensor(
                        out=uT[:, k, :], in0=pT[:, k, PAD + j:PAD + j + SEQ],
                        scalar=vecT[:, bass.ds(V_TAP + j * KC + k + d * KB, 1)], in1=uT[:, k, :],
                        op0=ALU.mult, op1=ALU.add)
                last.then_inc(tap_step, 1)

            def conv_low(d):
                dve.wait_ge(cu_hi, d + 1)
                V.tensor_tensor(cuT_lo[:, bass.ds(d * KB, KB), :], uT[:],
                                cuT_hi[:, bass.ds(d * KB, KB), :].bitcast(F32), ALU.subtract).then_inc(cu_lo, 1)

            def conv_0(d):
                dve.wait_ge(p_read, d + 1)
                tap(d, 1)

            def conv_1(d):
                dve.wait_ge(tap_step, d * 2 + 1)
                tap(d, 0)
                dve.wait_ge(tap_step, d * 2 + 2)
                dve.wait_ge(cb_out, d + 1)
                V.tensor_tensor(uT[:], uT[:], cbT[:], ALU.mult).then_inc(u_done, 1)

            def conv_turn(i):
                first = starts(i)

                def normalise(b, source, emc, dst, steps, done):
                    d = source[:, DV:DV + 1]
                    V.tensor_scalar(out=den[:, 0:1], in0=d, scalar1=head_cols[:, b, emc:emc + 1], scalar2=None,
                                    op0=ALU.max).then_inc(den_step, 1)
                    dve.wait_ge(den_step, steps + 1)
                    V.scalar_tensor_tensor(out=den[:, 1:2], in0=d, scalar=-1.0, in1=den[:, 0:1], op0=ALU.mult,
                                           op1=ALU.max).then_inc(den_step, 1)
                    dve.wait_ge(den_step, steps + 2)
                    V.reciprocal(den[:, 2:3], den[:, 1:2]).then_inc(den_step, 1)
                    dve.wait_ge(den_step, steps + 3)
                    V.tensor_scalar(out=dst, in0=source[:, 0:DV], scalar1=den[:, 2:3], scalar2=None,
                                    op0=ALU.mult).then_inc(done, 1)

                STEPS = 7

                def h_first(b):
                    dve.wait_ge(first_done, i * 2 + b + 1)
                    normalise(b, ps[:, 6, 0:DV + 1], EMC, vx[:, 0, i * 2 + b, 0:DV],
                              i * (2 * STEPS) + b * STEPS, h0_done)

                def h_second(b):
                    dve.wait_ge(inter_out, i * 2 + b + 1)
                    V.tensor_tensor(num[:], ps[:, 6, 0:DV + 1], inter[:], ALU.add).then_inc(den_step, 1)
                    dve.wait_ge(den_step, i * (2 * STEPS) + b * STEPS + 4)
                    normalise(b, num[:], EMC + 1, vx[:, 1, i * 2 + b, 0:DV],
                              i * (2 * STEPS) + b * STEPS + 4, h1_done)

                for j in range(3 * BC):
                    c = Chunk(G_CONV + j, i, 3 * BC)
                    split(c.next())
                    if j == 0 and not first:
                        conv_0(i - 1)
                    if j == 1:
                        if not first:
                            dve.wait_ge(scored, i * 2)
                        else:
                            dve.wait_ge(cols_turned, 1)
                        for b in range(2):
                            V.tensor_scalar(out=sel[b][:], in0=r_negM[:], scalar1=ident[0:H, bass.ds(i * 2 + b, 1)],
                                            scalar2=None, op0=ALU.mult).then_inc(selected, 1)
                        if not first:
                            conv_1(i - 1)
                    if j == 2 and not first:
                        conv_low(i - 1)
                    if j == 3:
                        for b in range(2):
                            dve.wait_ge(scored, i * 2 + b + 1)
                            V.tensor_tensor(head_w[:, b, :, :], ps[:, 6 + b, 2 * P:4 * P].rearrange("p (r t) -> p r t", r=RT),
                                            causal[:].rearrange("p (o t) -> p o t", o=1).to_broadcast([P, RT, P]),
                                            ALU.add).then_inc(weighed, 1)
                        for b in range(2):
                            dve.wait_ge(exped, i * 2 + b + 1)
                            if not first:
                                dve.wait_ge(second_done, i * 2)
                            V.tensor_tensor(head_sc[:, b, :, :], ps[:, 6 + b, 0:2 * P].rearrange("p (r t) -> p r t", r=RT),
                                            head_w[:, b, :, :], ALU.mult).then_inc(scores_done, 1)
                    if j == 4:
                        for b in range(2):
                            dve.wait_ge(staged, i * 2 + b + 1)
                            V.tensor_scalar(out=head_kw[:, b, :], in0=head_qk[:, b, 2, :],
                                            scalar1=head_cols[:, b, WK:WK + 1], scalar2=None,
                                            op0=ALU.mult).then_inc(kw_done, 1)
                    if j == 6:
                        h_first(0)
                    if j == 7:
                        h_second(0)
                    if j == 8:
                        h_first(1)
                    if j == 9:
                        h_second(1)
                dve.wait_ge(lo_used, c.count(1))
                dve.wait_ge(act_out, A_CONV + 2 + i * 2)
                V.tensor_tensor(nat[:], ps[:, 4:6, :], nat[:], ALU.mult).then_inc(dve_out, 1)

            conv_turn(0)
            with dve.Fori(1, NB) as i:
                conv_turn(i)

            for n in range(NB):
                for q in range(BC):
                    c = Chunk(G_O + n * BC + q)
                    split(c.next())
                    if n == 0 and q < 3:
                        (conv_0, conv_1, conv_low)[q](NB - 1)
                    if n > 0 and q == 1:
                        group_lo(GRP_HM + n, HI_HM + (n - 1) * KB, hmT_lo, hmT_hi, (n - 1) * KB, V_MH)
                dve.wait_ge(act_out, A_O + n + 1)
                if n == 0:
                    dve.wait_ge(h_rstd, 1)
                else:
                    dve.wait_ge(grp_turned, GRP_HM + n)
                for r in range(RT):
                    for b in range(2):
                        h = 2 * n + b
                        last = V.scalar_tensor_tensor(out=hm[:, r, b * DV:(b + 1) * DV], in0=vx[:, r, h, 0:DV],
                                                      scalar=rstd[:, r * H + h:r * H + h + 1],
                                                      in1=nat[:, r, b * DV:(b + 1) * DV], op0=ALU.mult, op1=ALU.mult)
                last.then_inc(hm_done, 1)

            def merge_turn(i):
                first = starts(i)
                for j in range(4 * BC):
                    c = Chunk(G_MERGE + j, i, 4 * BC)
                    split(c.next())
                    if j == 1:
                        if first:
                            group_lo(GRP_M, HI_HM + (NB - 1) * KB, hmT_lo, hmT_hi, (NB - 1) * KB, V_MH)
                        else:
                            group_lo(i + GRP_M, HI_M - 1 + i, mT_lo, mT_hi, (i - 1) * KB)
                    if j == 3 + BC:
                        dve.wait_ge(lo_used, c.count(1))
                        dve.wait_ge(act_out, A_MERGE + 1 + i * 2)
                        V.tensor_tensor(prod[:], ps[:, 2:4, :], gate[:], ALU.mult).then_inc(dve_out, 1)
                dve.wait_ge(lo_used, c.count(1))
                dve.wait_ge(act_out, A_MERGE + 2 + i * 2)
                if not first:
                    dve.wait_ge(grp_turned, i + GRP_M)
                V.tensor_tensor(merged[:], ps[:, 2:4, :], gate[:], ALU.mult).then_inc(dve_out, 1)
                dve.wait_ge(dve_out, V_MERGE + 2 + i * 2)
                V.tensor_tensor(merged[:], merged[:], prod[:], ALU.add).then_inc(m_done, 1)

            merge_turn(0)
            with dve.Fori(1, NB) as i:
                merge_turn(i)

            for n in range(NB):
                for q in range(BC):
                    c = Chunk(G_OUT + n * BC + q)
                    split(c.next())
                    if q == 1:
                        if n == 0:
                            group_lo(GRP_F, HI_M + NB - 1, mT_lo, mT_hi, (NB - 1) * KB)
                        else:
                            group_lo(GRP_F + n, HI_F + (n - 1) * KB, fT_lo, fT_hi, (n - 1) * KB, V_FN)
                dve.wait_ge(lo_used, c.count(1))
                if n == 0:
                    dve.wait_ge(x_again, 16)
                part = x1[:, :, n * COLS:(n + 1) * COLS]
                V.tensor_tensor(part, ps[:, 2 * (n % 2):2 * (n % 2) + 2, :], part, ALU.add).then_inc(dve_out, 1)

            def ffn_turn(i):
                first = starts(i)
                for j in range(2 * BC):
                    c = Chunk(G_FFN + j, i, 2 * BC)
                    split(c.next())
                    if first and j == 0:
                        dve.wait_ge(x1_squared, RT * NB)
                        V.tensor_reduce(sums[:], ss1[:], axis=AX.X, op=ALU.add).then_inc(x1_summed, 1)
                    if first and j == 1:
                        group_lo(GRP_F + NB, HI_F + (NB - 1) * KB, fT_lo, fT_hi, (NB - 1) * KB, V_FN)
                dve.wait_ge(lo_used, c.count(1))
                dve.wait_ge(act_out, A_FFN + 1 + i)
                if not first:
                    dve.wait_ge(act_turned, i)
                for r in range(RT):
                    last = V.scalar_tensor_tensor(out=merged[:, r, :], in0=ps[:, 2 + r, :], scalar=r_x[:, 1, r:r + 1],
                                                  in1=gate[:, r, :], op0=ALU.mult, op1=ALU.mult)
                last.then_inc(dve_out, 1)

            ffn_turn(0)
            with dve.Fori(1, FB) as i:
                ffn_turn(i)

            def stage(chunk):
                dve.wait_ge(a_hi_staged, chunk.count(1 - G_DOWN))
                if not (isinstance(chunk.turn, int) and chunk.count(0) < G_DOWN + 2):
                    dve.wait_ge(lo_used, chunk.count(-1))
                V.tensor_tensor(a_lo[:, chunk.split, :], actT[:, chunk.count(-G_DOWN), :],
                                a_hi[:, chunk.split, :].bitcast(F32), ALU.subtract).then_inc(a_lo_staged, 1)

            stage(Chunk(G_DOWN))

            def down_turn(i, last=False):
                for n in range(RAW_SLOTS):
                    c = Chunk(G_DOWN + n, i, RAW_SLOTS)
                    if not (last and n == RAW_SLOTS - 1):
                        split(c.next())
                        stage(c.next())

            down_turn(0)
            with dve.Fori(1, FC // RAW_SLOTS - 1) as i:
                down_turn(i)
            down_turn(FC // RAW_SLOTS - 1, last=True)

            for r in range(RT):
                dve.wait_ge(down_done, r + 1)
                V.tensor_tensor(x1[:, r, :], ps[:, 4 * r:4 * r + 4, :].rearrange("p b n -> p (b n)"), x1[:, r, :],
                                ALU.add).then_inc(y_sum, 1)
            dve.wait_ge(final_landed, 16)
            for r in range(RT):
                dve.wait_ge(y_rstd, r + 1)
                V.scalar_tensor_tensor(out=y[:, r, :], in0=x1[:, r, :], scalar=r_x[:, 0, r:r + 1], in1=g_final[:],
                                       op0=ALU.mult, op1=ALU.mult).then_inc(y_done, 1)

        @block.tensor
        def _(pe):
            T = nc.tensor

            def project(chunk, banks, hi, lo, q, after_hi=None):
                rows = lambda part, k, r: part[:, q * KB + k, r * P:(r + 1) * P]
                pe.wait_ge(hi_split, chunk.count(1))
                for k in range(KB):
                    w = w_hi[:, chunk.split, k * COLS:(k + 1) * COLS]
                    for r in range(RT):
                        T.matmul(ps[:, banks + r, :], rows(hi, k, r), w, start=(q == 0 and k == 0), stop=False)
                        last = T.matmul(ps[:, banks + r, :], rows(lo, k, r), w, start=False, stop=False)
                last.then_inc(hi_used, 1)
                pe.wait_ge(lo_split, chunk.count(1))
                for k in range(KB):
                    w = w_lo[:, chunk.split, k * COLS:(k + 1) * COLS]
                    for r in range(RT):
                        last = T.matmul(ps[:, banks + r, :], rows(hi, k, r), w, start=False,
                                        stop=(q == BC - 1 and k == KB - 1))
                last.then_inc(lo_used, 1)

            def turn_block(source, bank, done):
                for k in range(KB):
                    for r in range(RT):
                        at_col = (k % 2) * SEQ + r * P
                        last = T.transpose(ps[:, bank + k // 2, at_col:at_col + P],
                                           source[:, r, k * P:(k + 1) * P], ident[:])
                last.then_inc(done, 1)

            pe.wait_ge(setup, 3)
            pe.wait_ge(small_landed[0], 64)
            T.transpose(ps[:, 0, 0:96], vec_rows[:], ident[0:96, 0:96]).then_inc(vec_turned, 1)
            pe.wait_ge(x_normed, RT)
            for k2 in range(KC // 2):
                if k2 >= 4:
                    pe.wait_ge(x_lo_done, 2 * (k2 - 4) + 2)
                for k in range(2):
                    for r in range(RT):
                        last = T.transpose(ps[:, 4 + k2 % 4, k * SEQ + r * P:k * SEQ + (r + 1) * P],
                                           xn[:, r, (2 * k2 + k) * P:(2 * k2 + k + 1) * P], ident[:])
                last.then_inc(x_turned, 1)

            pe.wait_ge(vec_ready, 1)
            for q in range(BC):
                pe.wait_ge(x_lo_done, (q + 1) * KB)
                project(Chunk(G_QK + q), 0, xT_hi, xT_lo, q)
            for q in range(BC):
                project(Chunk(G_QK + BC + q), 2, xT_hi, xT_lo, q)

            def two_blocks(at_chunk, i, blocks_before):
                for n in range(2):
                    pe.wait_ge(act_out, blocks_before + n - 1 + i * 2)
                    for q in range(BC):
                        project(Chunk(at_chunk + n * BC + q, i, 2 * BC), 2 * n, xT_hi, xT_lo, q)

            with pe.Fori(1, 2) as i:
                two_blocks(G_QK, i, 0)

            pe.wait_ge(gw_lo, 1)
            for k in range(KC):
                T.matmul(ps[:, 6, 0:SEQ], wg_hi[:, k, :], xT_hi[:, k, :], start=(k == 0), stop=False)
                T.matmul(ps[:, 6, 0:SEQ], wg_hi[:, k, :], xT_lo[:, k, :], start=False, stop=False)
                last = T.matmul(ps[:, 6, 0:SEQ], wg_lo[:, k, :], xT_hi[:, k, :], start=False, stop=(k == KC - 1))
            last.then_inc(gates_done, 1)

            with pe.Fori(0, 2) as i:
                two_blocks(G_V, i, A_V)

            pe.wait_ge(rows_act, 3)
            for n, r in enumerate((r_a[:, 0, :], r_a[:, 1, :], r_wk[:, 0, :], r_int[:, 0, :], r_emc[:, 0, :],
                                   r_emc[:, 1, :])):
                last = T.matmul(ps[:, 7, n * H:(n + 1) * H], r, ident[0:H, 0:H], start=True, stop=True)
            last.then_inc(cols_turned, 1)

            def conv_turn(i):
                first = starts(i)

                def head_turn(b):
                    pe.wait_ge(staged, i * 2 + b + 1)
                    for n in range(4):
                        last = T.transpose(ps[:, 6 + b, n * P:(n + 1) * P], head_qk[:, b, n, :], ident[:])
                    last.then_inc(turned, 1)

                def head_scores(b):
                    pe.wait_ge(turned_out, i * 2 + b + 1)
                    pe.wait_ge(selected, i * 2 + b + 1)
                    for r in range(RT):
                        T.matmul(ps[:, 6 + b, r * P:(r + 1) * P], head_qkT[:, b, 2 + r, :], head_qkT[:, b, r, :],
                                 start=True, stop=True)
                    T.matmul(ps[:, 6 + b, 2 * P:4 * P], ones[:], sel[b][:], start=True, stop=True).then_inc(scored, 1)

                def head_first(b):
                    pe.wait_ge(scores_done, i * 2 + b + 1)
                    pe.wait_ge(kw_done, i * 2 + b + 1)
                    v = vx[:, 0, i * 2 + b, :]
                    T.matmul(ps[:, 6, 0:DV + 1], head_sc[:, b, 0, :], v, start=True, stop=True)
                    T.matmul(ps[:, 7, 0:DV + 1], head_kw[:, b, :], v, start=True, stop=True).then_inc(first_done, 1)

                def head_second(b):
                    pe.wait_ge(state_out, i * 2 + b + 1)
                    pe.wait_ge(h0_done, i * 2 + b + 1)
                    T.matmul(ps[:, 6, 0:DV + 1], head_sc[:, b, 1, :], vx[:, 1, i * 2 + b, :], start=True, stop=True)
                    T.matmul(ps[:, 7, 0:DV + 1], head_qkT[:, b, 1, :], head_C[:, b, :], start=True,
                             stop=True).then_inc(second_done, 1)

                for j in range(3 * BC):
                    if j == 0:
                        pe.wait_ge(act_out, A_CONV - 1 + i * 2)
                    if j == BC:
                        pe.wait_ge(act_out, A_CONV + i * 2)
                    if j == 2 * BC and not first:
                        pe.wait_ge(dve_out, i)
                    project(Chunk(G_CONV + j, i, 3 * BC), 2 * (j // BC), xT_hi, xT_lo, j % BC)
                    if j == 0 and not first:
                        turn_p(i - 1)
                    if j == 2:
                        if first:
                            pe.wait_ge(cols_ready, 1)
                        else:
                            pe.wait_ge(p_read, i)
                        head_turn(0)
                        head_turn(1)
                    if j == 3:
                        head_scores(0)
                        head_scores(1)
                    if j == 5:
                        pe.wait_ge(act_out, A_CONV + 1 + i * 2)
                        pe.wait_ge(scores_done, i * 2 + 2)
                        turn_block(nat, 6, cb_turned)
                    if j == 6:
                        pe.wait_ge(cb_out, i + 1)
                        head_first(0)
                    if j == 7:
                        head_second(0)
                    if j == 8:
                        pe.wait_ge(h1_done, i * 2 + 1)
                        head_first(1)
                    if j == 9:
                        head_second(1)

            def turn_p(d):
                pe.wait_ge(dve_out, d + 1)
                pe.wait_ge(h1_done, d * 2 + 2)
                turn_block(nat, 6, p_turned)

            conv_turn(0)
            with pe.Fori(1, NB) as i:
                conv_turn(i)

            for n in range(NB):
                pe.wait_ge(act_out, A_O - 1 + n)
                for q in range(BC):
                    project(Chunk(G_O + n * BC + q), 2 * (n % 2), xT_hi, xT_lo, q)
                    if n == 0 and q == 0:
                        turn_p(NB - 1)
                    if n > 0 and q == 1:
                        pe.wait_ge(hm_done, n)
                        if n > 1:
                            pe.wait_ge(grp_lo, n - 1)
                        turn_block(hm, 4, grp_turned)

            def merge_turn(i):
                first = starts(i)
                for j in range(4 * BC):
                    q = j % BC
                    if j == 0:
                        pe.wait_ge(act_out, A_MERGE - 1 if first else A_MERGE + i * 2)
                    if j == BC:
                        if first:
                            pe.wait_ge(act_out, A_MERGE)
                        else:
                            pe.wait_ge(dve_out, V_MERGE + i * 2)
                    if j == 2 * BC:
                        pe.wait_ge(act_out, A_MERGE + 1 + i * 2)
                    if j == 3 * BC:
                        pe.wait_ge(dve_out, V_MERGE + 1 + i * 2)
                    if first and j == 2 * BC - 1:
                        pe.wait_ge(grp_lo, GRP_M)
                    if first and j == 3 * BC:
                        pe.wait_ge(cu_lo, NB)
                    hi, lo = {1: (hmT_hi, hmT_lo), 3: (cuT_hi, cuT_lo)}.get(j // BC, (xT_hi, xT_lo))
                    project(Chunk(G_MERGE + j, i, 4 * BC), 2 * (j // BC % 2), hi, lo, q)
                    if j == 1:
                        if first:
                            pe.wait_ge(hm_done, NB)
                            pe.wait_ge(grp_lo, GRP_M - 1)
                            turn_block(hm, 4, grp_turned)
                        else:
                            pe.wait_ge(m_done, i)
                            pe.wait_ge(grp_lo, GRP_M - 1 + i)
                            turn_block(merged, 4, grp_turned)

            merge_turn(0)
            with pe.Fori(1, NB) as i:
                merge_turn(i)

            for n in range(NB):
                if n == 0:
                    pe.wait_ge(act_out, A_FFN)
                else:
                    pe.wait_ge(dve_out, V_OUT + n - 1)
                for q in range(BC):
                    if n == 0 and q == BC - 1:
                        pe.wait_ge(grp_lo, GRP_F)
                    project(Chunk(G_OUT + n * BC + q), 2 * (n % 2), mT_hi, mT_lo, q)
                    if q == 1:
                        if n == 0:
                            pe.wait_ge(m_done, NB)
                            pe.wait_ge(grp_lo, GRP_F - 1)
                            turn_block(merged, 4, grp_turned)
                        else:
                            pe.wait_ge(grp_lo, GRP_F + n - 1)
                            turn_block(x1[:, :, (n - 1) * COLS:n * COLS], 4, grp_turned)

            def turn_act(d):
                pe.wait_ge(dve_out, V_FFN + 1 + d)
                if not starts(d):
                    pe.wait_ge(act_out_of, d)
                turn_block(merged, 4, act_turned)

            def ffn_turn(i, d=None):
                first = starts(i)
                for j in range(2 * BC):
                    if j == 0:
                        pe.wait_ge(*((dve_out, V_FFN - 1) if first else (act_out, A_FFN + i)))
                    if j == BC:
                        pe.wait_ge(dve_out, V_FFN + i)
                    if first and j == BC - 1:
                        pe.wait_ge(grp_lo, GRP_F + NB)
                    project(Chunk(G_FFN + j, i, 2 * BC), 2 * (j // BC), fT_hi, fT_lo, j % BC)
                    if j == 1:
                        if first:
                            pe.wait_ge(dve_out, V_FFN)
                            pe.wait_ge(grp_lo, GRP_F + NB - 1)
                            turn_block(x1[:, :, (NB - 1) * COLS:NB * COLS], 4, grp_turned)
                        else:
                            turn_act(i - 1)

            ffn_turn(0)
            ffn_turn(1)
            with pe.Fori(2, FB) as i:
                ffn_turn(i)
            turn_act(FB - 1)

            def down(chunk, first, last):
                h, l = a_hi[:, chunk.split, :], a_lo[:, chunk.split, :]
                wh = [w_hi[:, chunk.split, n * COLS:(n + 1) * COLS] for n in range(4)]
                wl = [w_lo[:, chunk.split, n * COLS:(n + 1) * COLS] for n in range(4)]
                tile = lambda part, r: part[:, r * P:(r + 1) * P]

                def high(r):
                    for n in range(4):
                        T.matmul(ps[:, 4 * r + n, :], tile(h, r), wh[n], start=first, stop=False)
                    for n in range(4):
                        ins = T.matmul(ps[:, 4 * r + n, :], tile(l, r), wh[n], start=False, stop=False)
                    return ins

                def low(r):
                    for n in range(4):
                        ins = T.matmul(ps[:, 4 * r + n, :], tile(h, r), wl[n], start=False, stop=last)
                    return ins

                pe.wait_ge(hi_split, chunk.count(1))
                pe.wait_ge(a_lo_staged, chunk.count(1 - G_DOWN))
                if last:
                    high(0)
                    pe.wait_ge(lo_split, chunk.count(1))
                    low(0).then_inc(down_done, 1)
                    high(1)
                    low(1).then_inc(down_done, 1)
                    return
                high(0)
                if first:
                    pe.wait_ge(act_out_of, FB)
                high(1).then_inc(hi_used, 1)
                pe.wait_ge(lo_split, chunk.count(1))
                low(0)
                low(1).then_inc(lo_used, 1)

            pe.wait_ge(act_out, A_FFN + FB)
            pe.wait_ge(dve_out, V_FFN + FB)
            for n in range(RAW_SLOTS):
                down(Chunk(G_DOWN + n), first=(n == 0), last=False)
            with pe.Fori(1, FC // RAW_SLOTS - 1) as i:
                for n in range(RAW_SLOTS):
                    down(Chunk(G_DOWN + n, i, RAW_SLOTS), first=False, last=False)
            for n in range(RAW_SLOTS):
                down(Chunk(G_DOWN + n, FC // RAW_SLOTS - 1, RAW_SLOTS), first=False, last=(n == RAW_SLOTS - 1))


_INS = ["x", "norm_mix", "w_in", "b_igate", "b_fgate", "conv_w", "mh_norm", "w_branch_a", "w_branch_b",
        "w_out", "norm_ffn", "w_gate", "w_up", "w_down", "norm_final"]


def kernel(**inputs):
    import concourse.bacc as bacc
    from concourse.bass_utils import run_bass_kernel_spmd

    nc = bacc.Bacc("TRN2", target_bir_lowering=False, num_devices=1)
    arrays, args = {}, []
    for name in _INS:
        a = np.ascontiguousarray(inputs[name])
        arrays[f"in_{name}"] = a
        args.append(nc.dram_tensor(f"in_{name}", a.shape, mybir.dt.from_np(a.dtype), kind="ExternalInput").ap())
    out = nc.dram_tensor("out_y", inputs["x"].shape, F32, kind="ExternalOutput").ap()
    hybrid_block(nc, *args, out)
    r = run_bass_kernel_spmd(nc, [arrays], core_ids=[0])
    return r.results[0]["out_y"]
```

```python
from contextlib import ExitStack

import numpy as np

import concourse.bass as bass
from concourse import mybir

ALU = mybir.AluOpType
ACT = mybir.ActivationFunctionType
AX = mybir.AxisListType
F32 = mybir.dt.float32
F32R = mybir.dt.float32r

P = 128
COLS = 512
RAW_SLOTS = 4
SPLIT_SLOTS = 2
KB = 4
MASKED = -1e30


def starts(turn):
    return isinstance(turn, int) and turn == 0


class Chunk:

    def __init__(self, at, turn=0, stride=0):
        self.at, self.turn, self.stride = at, turn, stride

    def count(self, more):
        return self.at + more + self.turn * self.stride

    def landed(self):
        return 16 * (self.at // RAW_SLOTS + 1) + self.turn * (16 * self.stride // RAW_SLOTS)

    def next(self):
        return Chunk(self.at + 1, self.turn, self.stride)

    @property
    def raw(self):
        return self.at % RAW_SLOTS

    @property
    def split(self):
        return self.at % SPLIT_SLOTS


def hybrid_block(nc, x, norm_mix, w_in, b_igate, b_fgate, conv_w, mh_norm, w_branch_a, w_branch_b,
                 w_out, norm_ffn, w_gate, w_up, w_down, norm_final, out):
    _, SEQ, D = x.shape
    H = b_igate.shape[1]
    DK, DV = D // 16, D // 8
    CHUNK = 128
    RT = SEQ // P
    KC = D // P
    F = w_gate.shape[2]
    FC = F // P
    NB = D // COLS
    FB = F // COLS
    TAPS = conv_w.shape[1]
    EPS = 1e-6
    QK_SCALE = float(DK) ** -0.5
    assert RT == 2 and CHUNK == P and DK == P and KC == 16 and NB == 4 and TAPS == 3

    C_QK, C_V, C_O = 0, 2 * H * DK, 2 * H * DK + H * DV
    C_GATES = C_O + H * DV
    C_CB = C_GATES + 2 * H
    C_CC, C_CX = C_CB + D, C_CB + 2 * D
    C_GA, C_GB = C_CB + 3 * D, C_CB + 4 * D

    BC = KC // KB
    G_QK = 0
    G_V = G_QK + 4 * BC
    G_CONV = G_V + 4 * BC
    G_O = G_CONV + 3 * NB * BC
    G_MERGE = G_O + NB * BC
    G_OUT = G_MERGE + 4 * NB * BC
    G_FFN = G_OUT + NB * BC
    G_DOWN = G_FFN + 2 * FB * BC
    G_END = G_DOWN + FC

    A_V, A_CONV = 4, 8
    A_O = A_CONV + 2 * NB
    A_MERGE = A_O + NB
    A_FFN = A_MERGE + 2 * NB
    V_MERGE = NB
    V_OUT = V_MERGE + 2 * NB
    V_FFN = V_OUT + NB

    flat = lambda w: w.rearrange("o k n -> (o k) n")
    by_k = lambda w: flat(w).rearrange("(k p) n -> p k n", p=P)
    x_rows = x.rearrange("b (r p) d -> p (b r) d", p=P)
    out_rows = out.rearrange("b (r p) d -> p (b r) d", p=P)
    w_in_k, w_a_k, w_b_k, w_out_k = by_k(w_in), by_k(w_branch_a), by_k(w_branch_b), by_k(w_out)
    w_gate_k, w_up_k, w_down_k = by_k(w_gate), by_k(w_up), by_k(w_down)

    with ExitStack() as ctx:
        BASE = -(-nc.sbuf_base // 64) * 64
        CH = KB * COLS * 4
        AT = KC * SEQ * 4
        RING = BASE
        R1 = RING + (RAW_SLOTS + 2 * SPLIT_SLOTS) * CH
        R2 = R1 + 2 * AT
        R3 = R2 + 2 * AT
        Z = R3 + 2 * AT

        def at(name, shape, dt, offset):
            return nc.alloc_sbuf_tensor_at(name, shape, dt, offset=offset)

        w_raw = at("w_raw", [P, RAW_SLOTS, CH // 4], F32, RING)
        w_hi = at("w_hi", [P, SPLIT_SLOTS, CH // 4], F32R, RING + RAW_SLOTS * CH)
        w_lo = at("w_lo", [P, SPLIT_SLOTS, CH // 4], F32R, RING + (RAW_SLOTS + SPLIT_SLOTS) * CH)

        xT_hi, xT_lo = at("xT_hi", [P, KC, SEQ], F32R, R1), at("xT_lo", [P, KC, SEQ], F32R, R1 + AT)
        cuT_hi, cuT_lo = at("cuT_hi", [P, KC, SEQ], F32R, R2), at("cuT_lo", [P, KC, SEQ], F32R, R2 + AT)
        hmT_hi, hmT_lo = at("hmT_hi", [P, KC, SEQ], F32R, R3), at("hmT_lo", [P, KC, SEQ], F32R, R3 + AT)
        xn = at("xn", [P, RT, D], F32, R2)
        wg = at("wg", [P, KC, P], F32R, R2 + AT)
        qk = at("qk", [P, RT, 2 * H * DK], F32, R3)
        s = R3 + RT * 2 * H * DK * 4
        head_qk = at("head_qk", [P, 2, 4, P], F32, s)
        head_qkT = at("head_qkT", [P, 2, 4, P], F32, s + 4096)
        head_w = at("head_w", [P, 2, RT, P], F32, s + 8192)
        head_sc = at("head_sc", [P, 2, RT, P], F32, s + 10240)
        head_kw = at("head_kw", [P, 2, P], F32, s + 12288)
        head_C = at("head_C", [P, 2, DV + 1], F32, s + 13312)
        actT = at("actT", [P, FC, SEQ], F32, R1)
        x1 = at("x1", [P, RT, D], F32, R2 + AT)
        assert R1 + FC * SEQ * 4 <= R2 + AT
        fT_hi, fT_lo = at("fT_hi", [P, KC, SEQ], F32R, R3), at("fT_lo", [P, KC, SEQ], F32R, R3 + AT)

        VX = RT * H * (DV + 1) * 4
        vx = at("vx", [P, RT, H, DV + 1], F32, Z)
        sq_x = at("sq_x", [P, D], F32, Z)
        vec_rows = at("vec_rows", [96, P], F32, Z + 8192)
        wg_raw = at("wg_raw", [P, KC, 2 * H], F32, Z + 8192 + 512)
        s = Z + VX
        nat = at("nat", [P, RT, COLS], F32, s)
        pT = at("pT", [P, KB, SEQ + 32], F32, s + 4096)
        PAD = 32 - (TAPS - 1)
        diag = at("diag", [P, RT, P], F32, s)
        r_row = at("r_row", [P, SEQ], F32, s + 1024)
        ones_p = at("ones_p", [P, P], F32, s + 2048)
        s += 4096 + KB * (SEQ + 32) * 4
        uT = at("uT", [P, KB, SEQ], F32, s)
        cbT = at("cbT", [P, KB, SEQ], F32, s + 4096)
        hm = at("hm", [P, RT, COLS], F32, s + 4096)
        s += 8192
        row = lambda name, k, n=RT: at(name, [H, n, P], F32, s + 1024 * k)
        r_a, r_lf, r_t, r_b, r_M, r_bM, r_negM = (row(n, k) for k, n in enumerate(
            ["r_a", "r_lf", "r_t", "r_b", "r_M", "r_bM", "r_negM"]))
        r_emc, r_wk, r_int = row("r_emc", 7), row("r_wk", 8, 1), at("r_int", [H, 1, P], F32, s + 8704)
        neg = at("neg", [64, RT, P], F32R, s + 1024 * 2)
        sel = [at(f"sel{b}", [64, RT, P], F32R, s + 1024 * b) for b in range(2)]
        s += 9216
        inter = at("inter", [P, DV + 1], F32, s)
        num = at("num", [P, DV + 1], F32, s + 1056)
        mT_hi, mT_lo = at("mT_hi", [P, KC, SEQ], F32R, Z), at("mT_lo", [P, KC, SEQ], F32R, Z + AT)
        gate = at("gate", [P, RT, COLS], F32, Z + 2 * AT)
        prod = at("prod", [P, RT, COLS], F32, Z + 2 * AT + 4096)
        merged = at("merged", [P, RT, COLS], F32, Z + 2 * AT + 8192)
        g_final = at("g_final", [P, D], F32, Z)
        y = at("y", [P, RT, D], F32, Z + D * 4)
        sq_y = at("sq_y", [P, D], F32, Z + 3 * D * 4)
        CONST = Z + 2 * AT + 12288
        assert s + 2 * 1056 <= CONST, (s, CONST)
        s = CONST
        ident = at("ident", [P, P], F32, s)
        causal = at("causal", [P, P], F32, s + 512)
        vecT = at("vecT", [P, 96], F32, s + 1024)
        ones = at("ones", [64, P], F32R, s + 1408)
        cols = at("cols", [P, 6, H], F32, s + 1920)
        head_cols = at("head_cols", [P, 2, 6], F32, s + 2112)
        gate_bias = at("gate_bias", [H, 2], F32, s + 2176)
        half = at("half", [P, 2 * H], F32, s + 2208)
        ss = at("ss", [P, 2 * H], F32, s + 2272)
        rstd = at("rstd", [P, 2 * H], F32, s + 2336)
        ss1 = at("ss1", [P, RT, NB], F32, s + 2400)
        ssx = at("ssx", [P, 2, RT], F32, s + 2432)
        r_x = at("r_x", [P, 2, RT], F32, s + 2464)
        den = at("den", [P, 4], F32, s + 2496)
        sums = at("sums", [P, RT], F32, s + 2528)
        a_hi = at("a_hi", [P, 2, SEQ], F32R, CONST - 8192)
        a_lo = at("a_lo", [P, 2, SEQ], F32R, CONST - 8192 + 2048)
        pick = at("pick", [64, H], F32, s + 2560)
        assert s + 2592 <= nc.sbuf_usable_end, (s + 2592, nc.sbuf_usable_end)
        A_IN, WK, INT, EMC = 0, 2, 3, 4
        V_MIX, V_MH, V_FN, V_TAP = 0, KC, 2 * KC, 3 * KC

        ps = ctx.enter_context(nc.psum_tensor("ps", [P, 8, COLS], F32))

        def sem(name):
            return ctx.enter_context(nc.semaphore(name))

        raw_landed = [sem(f"raw_landed{n}") for n in range(RAW_SLOTS)]
        half_landed, half_hi = sem("half_landed"), sem("half_hi")
        hi_split, lo_split = sem("hi_split"), sem("lo_split")
        hi_used, lo_used = sem("hi_used"), sem("lo_used")
        act_out, dve_out = sem("act_out"), sem("dve_out")
        x_landed = [sem(f"x_landed{n}") for n in range(NB)]
        small_landed = [sem(f"small_landed{n}") for n in range(4)]
        x_again, final_landed, stored = sem("x_again"), sem("final_landed"), [sem("stored0"), sem("stored1")]
        setup, setup2 = sem("setup"), sem("setup2")
        x_squared, x_mean, x_rstd, diag_done = sem("x_squared"), sem("x_mean"), sem("x_rstd"), sem("diag_done")
        vec_turned, vec_ready = sem("vec_turned"), sem("vec_ready")
        x_turned, x_hi_done, x_lo_done = sem("x_turned"), sem("x_hi_done"), sem("x_lo_done")
        gw_hi, gw_lo, gates_done = sem("gw_hi"), sem("gw_lo"), sem("gates_done")
        neg_hi, neg_lo = sem("neg_hi"), sem("neg_lo")
        rows_dve, rows_act = sem("rows_dve"), sem("rows_act")
        cols_turned, cols_ready = sem("cols_turned"), sem("cols_ready")
        staged, turned, turned_out = sem("staged"), sem("turned"), sem("turned_out")
        selected, scored, weighed, exped, scores_done = (sem("selected"), sem("scored"), sem("weighed"),
                                                         sem("exped"), sem("scores_done"))
        kw_done, first_done, state_out, h0_done = sem("kw_done"), sem("first_done"), sem("state_out"), sem("h0_done")
        second_done, inter_out = sem("second_done"), sem("inter_out")
        h1_done, den_step = sem("h1_done"), sem("den_step")
        cb_turned, cb_out = sem("cb_turned"), sem("cb_out")
        p_turned, p_copied, p_read = sem("p_turned"), sem("p_copied"), sem("p_read")
        tap_step, u_done, cu_hi, cu_lo = sem("tap_step"), sem("u_done"), sem("cu_hi"), sem("cu_lo")
        h_squared, h_mean, h_rstd, hm_done = sem("h_squared"), sem("h_mean"), sem("h_rstd"), sem("hm_done")
        grp_turned, grp_hi, grp_lo = sem("grp_turned"), sem("grp_hi"), sem("grp_lo")
        m_done, x1_squared, x1_summed, x1_mean, x1_rstd = (sem("m_done"), sem("x1_squared"), sem("x1_summed"),
                                                           sem("x1_mean"), sem("x1_rstd"))
        act_turned, act_out_of = sem("act_turned"), sem("act_out_of")
        a_hi_staged, a_lo_staged = sem("a_hi_staged"), sem("a_lo_staged")
        down_done, y_sum, y_squared, y_total = sem("down_done"), sem("y_sum"), sem("y_squared"), sem("y_total")
        y_mean, y_rstd, y_gained = sem("y_mean"), sem("y_rstd"), sem("y_gained")
        y_left, y_right = sem("y_left"), sem("y_right")

        block = ctx.enter_context(nc.Block())

        GRP_HM, GRP_M, GRP_F = 0, NB, 2 * NB
        HI_HM, HI_M, HI_F = 0, NB * KB, NB * KB + NB

        @block.sync
        def _(sp):
            def load(chunk, source):
                if not (isinstance(chunk.turn, int) and chunk.count(0) < RAW_SLOTS):
                    sp.wait_ge(lo_split, chunk.count(1 - RAW_SLOTS))
                dst = w_raw[:, chunk.raw, :]
                if len(source.shape) == 3:
                    dst = dst.rearrange("p (k n) -> p k n", k=KB)
                sp.dma_start(dst, source).then_inc(raw_landed[chunk.raw], 16)

            def load_block(at_chunk, turn, stride, w, col):
                for q in range(BC):
                    load(Chunk(at_chunk + q, turn, stride), w[:, q * KB:(q + 1) * KB, bass.ds(col, COLS)])

            kp = lambda v: v.rearrange("o (k p) -> (o k) p", p=P)
            def load_x(g):
                sp.dma_start(xn[:, :, g * COLS:(g + 1) * COLS],
                             x_rows[:, :, g * COLS:(g + 1) * COLS]).then_inc(x_landed[g], 16)

            sp.dma_start(vec_rows[V_MIX:V_MIX + KC, :], kp(norm_mix)).then_inc(small_landed[0], 16)
            load_x(0)
            sp.dma_start(vec_rows[V_MH:V_MH + KC, :], kp(mh_norm)).then_inc(small_landed[0], 16)
            sp.dma_start(vec_rows[V_FN:V_FN + KC, :], kp(norm_ffn)).then_inc(small_landed[0], 16)
            sp.dma_start(vec_rows[V_TAP:V_TAP + TAPS * KC, :],
                         conv_w.rearrange("o j (k p) -> (o j k) p", p=P)).then_inc(small_landed[0], 16)
            for q in range(BC):
                if q == 0:
                    for b in range(2):
                        part = w_raw[:, 0, b * CH // 8:(b + 1) * CH // 8]
                        sp.dma_start(part.rearrange("p (k n) -> p k n", k=KB // 2),
                                     w_in_k[:, b * KB // 2:(b + 1) * KB // 2, C_QK:C_QK + COLS]).then_inc(
                                         (half_landed, raw_landed[0])[b], 16)
                else:
                    load(Chunk(G_QK + q), w_in_k[:, q * KB:(q + 1) * KB, C_QK:C_QK + COLS])
                if q + 1 < NB:
                    load_x(q + 1)
            sp.dma_start(wg_raw[:], w_in_k[:, :, C_GATES:C_GATES + 2 * H]).then_inc(small_landed[1], 16)
            sp.dma_start(gate_bias[:, 0:1], b_igate.rearrange("o h -> h o")).then_inc(small_landed[2], 16)
            sp.dma_start(gate_bias[:, 1:2], b_fgate.rearrange("o h -> h o")).then_inc(small_landed[2], 16)
            load_block(G_QK + BC, 0, 0, w_in_k, C_QK + COLS)
            for n in range(2, 4):
                load_block(G_QK + n * BC, 0, 0, w_in_k, C_QK + n * COLS)
            with sp.Fori(0, 4) as i:
                load_block(G_V, i, BC, w_in_k, C_V + i * COLS)
            with sp.Fori(0, NB) as i:
                for n, c in enumerate((C_CB, C_CC, C_CX)):
                    load_block(G_CONV + n * BC, i, 3 * BC, w_in_k, c + i * COLS)
            with sp.Fori(0, NB) as i:
                load_block(G_O, i, BC, w_in_k, C_O + i * COLS)
            with sp.Fori(1, NB + 1) as i:
                for n, (w, c) in enumerate(((w_in_k, C_GA), (w_a_k, 0), (w_in_k, C_GB), (w_b_k, 0))):
                    load_block(G_MERGE + (n - 4) * BC, i, 4 * BC, w, i * COLS + (c - COLS))
            load_block(G_OUT, 0, 0, w_out_k, 0)
            load(Chunk(G_OUT + BC), w_out_k[:, 0:KB, COLS:2 * COLS])
            sp.wait_ge(lo_used, G_OUT)
            sp.dma_start(x1[:], x_rows).then_inc(x_again, 16)
            for q in range(1, BC):
                load(Chunk(G_OUT + BC + q), w_out_k[:, q * KB:(q + 1) * KB, COLS:2 * COLS])
            with sp.Fori(2, NB) as i:
                load_block(G_OUT, i, BC, w_out_k, i * COLS)

            def load_ffn(i):
                load_block(G_FFN, i, 2 * BC, w_gate_k, i * COLS)
                load_block(G_FFN + BC, i, 2 * BC, w_up_k, i * COLS)

            load_ffn(0)
            sp.wait_ge(lo_used, G_FFN)
            sp.dma_start(g_final[:], norm_final.rearrange("(a n) -> a n", a=1).to_broadcast([P, D])).then_inc(
                final_landed, 16)
            with sp.Fori(1, FB) as i:
                load_ffn(i)
            with sp.Fori(0, FC // RAW_SLOTS) as i:
                for n in range(RAW_SLOTS):
                    load(Chunk(G_DOWN + n, i, RAW_SLOTS), w_down_k[:, i * RAW_SLOTS + n, :])
            for r in range(RT):
                for n in range(NB // 2):
                    for done, c in ((y_right, (NB // 2 + n) * COLS), (y_left, n * COLS)):
                        sp.wait_ge(done, r * (NB // 2) + n + 1)
                        sp.dma_start(out_rows[:, r, c:c + COLS], y[:, r, c:c + COLS]).then_inc(stored[r], 16)
            for r in range(RT):
                sp.wait_ge(stored[r], 16 * NB)

        @block.gpsimd
        def _(pool):
            pool.memset(ident[:], 0.0).then_inc(setup, 1)
            pool.memset(causal[:], 0.0).then_inc(setup, 1)
            pool.wait_ge(setup, 2)
            pool.affine_select(out=ident[:], in_=ident[:], compare_op=ALU.not_equal, fill=1.0, base=0,
                               pattern=[[-1, P]], channel_multiplier=1).then_inc(setup, 1)
            pool.memset(half[:], -0.5).then_inc(setup, 1)
            pool.memset(ones[:].bitcast(F32), 1.0).then_inc(setup2, 1)
            pool.affine_select(out=causal[:], in_=causal[:], compare_op=ALU.is_ge, fill=MASKED, base=0,
                               pattern=[[1, P]], channel_multiplier=-1).then_inc(setup2, 1)
            pool.memset(ones_p[:], 1.0).then_inc(setup2, 1)
            pool.memset(wg[:].bitcast(F32), 0.0).then_inc(setup2, 1)
            pool.memset(neg[:].bitcast(F32), 0.0).then_inc(setup2, 1)

            def rstd_of(mean, source, total, result, squared, width, done):
                nc.gpsimd.tensor_scalar(out=total, in0=source, scalar1=1.0 / width, scalar2=EPS,
                                        op0=ALU.mult, op1=ALU.add).then_inc(mean, 1)
                pool.wait_ge(mean, squared)
                nc.gpsimd.tensor_tensor(out=result, in0=total, in1=half[:, 0:result.shape[1]],
                                        op=ALU.pow).then_inc(done, 1)

            pool.wait_ge(setup, 4)
            for r in range(RT):
                pool.wait_ge(x_squared, r + 1)
                rstd_of(x_mean, ssx[:, 0, r:r + 1], ssx[:, 1, r:r + 1], r_x[:, 0, r:r + 1], r + 1, D, x_rstd)
            pool.wait_ge(x_lo_done, KC)
            pool.wait_ge(gw_lo, 1)
            pool.memset(vx[:, :, :, DV:DV + 1], 1.0).then_inc(setup2, 1)
            pool.memset(pT[:, :, PAD:PAD + TAPS - 1], 0.0).then_inc(setup2, 1)

            qk_heads = qk[:].rearrange("p r (g n) -> p g r n", g=2)

            def stage(i):
                for b in range(2):
                    if not starts(i):
                        pool.wait_ge(h1_done, i * 2 + b - 1)
                    nc.gpsimd.tensor_copy(head_qk[:, b, :, :].rearrange("p (g r) n -> p g r n", g=2),
                                          qk_heads[:, :, :, bass.ds((i * 2 + b) * DK, DK)])
                    nc.gpsimd.tensor_copy(head_cols[:, b, :], cols[:, :, i * 2 + b]).then_inc(staged, 1)

            pool.wait_ge(act_out, A_V)
            pool.wait_ge(cols_ready, 1)
            stage(0)
            with pool.Fori(1, NB) as i:
                stage(i)

            pool.wait_ge(h_squared, RT * H)
            rstd_of(h_mean, ss[:], ss[:], rstd[:], 1, DV, h_rstd)
            pool.wait_ge(x1_summed, 1)
            rstd_of(x1_mean, sums[:], sums[:], r_x[:, 1, :], 1, D, x1_rstd)
            for r in range(RT):
                pool.wait_ge(y_total, r + 1)
                rstd_of(y_mean, sums[:, r:r + 1], ssx[:, 1, r:r + 1], r_x[:, 0, r:r + 1], r + 1, D, y_rstd)

        @block.scalar
        def _(act):
            copy = lambda o, i, **kw: nc.scalar.activation(o, i, ACT.Copy, **kw)

            def split(chunk):
                act.wait_ge(raw_landed[chunk.raw], chunk.landed())
                if not (isinstance(chunk.turn, int) and chunk.count(0) < SPLIT_SLOTS):
                    act.wait_ge(hi_used, chunk.count(1 - SPLIT_SLOTS))
                    act.wait_ge(lo_split, chunk.count(1 - SPLIT_SLOTS))
                copy(w_hi[:, chunk.split, :], w_raw[:, chunk.raw, :]).then_inc(hi_split, 1)

            def take(chunk, pair, dst, func=ACT.Copy):
                act.wait_ge(lo_used, chunk.count(1))
                for r in range(RT):
                    last = nc.scalar.activation(dst[:, r, :], ps[:, 2 * pair + r, :], func, scale=r_x[:, 0, r:r + 1])
                last.then_inc(act_out, 1)

            bank_kt = lambda b0: ps[:, b0:b0 + 2, :].rearrange("p b (k t) -> p (b k) t", k=2)

            def group_hi(n, dst, k0, step, scale_at=None):
                act.wait_ge(grp_turned, n)
                src = bank_kt(4)
                if scale_at is None:
                    copy(dst[:, bass.ds(k0, KB), :], src).then_inc(grp_hi, 1)
                    return
                for k in range(KB):
                    c = scale_at + k0 + k
                    copy(dst[:, k0 + k, :], src[:, k, :], scale=vecT[:, c:c + 1]).then_inc(grp_hi, 1)

            def x_high(g, ks=range(KB)):
                for k in ks:
                    if k % 2 == 0:
                        act.wait_ge(x_turned, 2 * g + k // 2 + 1)
                    c = g * KB + k
                    copy(xT_hi[:, c, :], bank_kt(4 + 2 * (g % 2))[:, k, :],
                         scale=vecT[:, V_MIX + c:V_MIX + c + 1]).then_inc(x_hi_done, 1)

            act.wait_ge(vec_turned, 1)
            copy(vecT[:], ps[:, 2, 0:96]).then_inc(vec_ready, 1)
            act.wait_ge(vec_ready, 1)
            x_high(0, range(2))
            act.wait_ge(half_landed, 16)
            copy(w_hi[:, 0, 0:CH // 8], w_raw[:, 0, 0:CH // 8]).then_inc(half_hi, 1)
            x_high(0, range(2, KB))
            act.wait_ge(raw_landed[0], 16)
            copy(w_hi[:, 0, CH // 8:], w_raw[:, 0, CH // 8:]).then_inc(hi_split, 1)

            def qk_turn(i):
                for n in range(2):
                    for q in range(BC):
                        c = Chunk(G_QK + n * BC + q, i, 2 * BC)
                        split(c.next())
                    take(c, n, qk[:, :, bass.ds((i * 2 + n) * COLS, COLS)])

            for q in range(BC):
                c = Chunk(G_QK + q)
                if q >= 2:
                    split(c.next())
                if q + 1 < NB:
                    x_high(q + 1)
                if q < 2:
                    split(c.next())
                if q >= BC - RT:
                    r = q - (BC - RT)
                    act.wait_ge(x_landed[NB - 1], 16)
                    if r > 0:
                        act.wait_ge(x_squared, r)
                    nc.scalar.activation(sq_x[:], xn[:, r, :], ACT.Square,
                                         accum_out=ssx[:, 0, r:r + 1]).then_inc(x_squared, 1)
                if q == 3:
                    act.wait_ge(small_landed[1], 16)
                    act.wait_ge(setup2, 5)
                    copy(wg[:, :, 0:64].rearrange("p k (g c) -> p k g c", g=2)[:, :, :, 0:H],
                         wg_raw[:].rearrange("p k (g c) -> p k g c", g=2)).then_inc(gw_hi, 1)
            act.wait_ge(x_rstd, RT)
            take(c, 0, qk[:, :, 0:COLS])
            for q in range(BC):
                c = Chunk(G_QK + BC + q)
                split(c.next())
            take(c, 1, qk[:, :, COLS:2 * COLS])
            with act.Fori(1, 2) as i:
                qk_turn(i)

            def gate_rows_1():
                act.wait_ge(rows_dve, 8)
                nc.scalar.activation(r_t[:], r_t[:], ACT.Exp).then_inc(rows_act, 1)
                act.wait_ge(rows_act, 1)
                nc.scalar.activation(r_t[:], r_t[:], ACT.Ln, bias=1.0).then_inc(rows_act, 1)

            def gate_rows_2():
                act.wait_ge(rows_dve, 17)
                nc.scalar.activation(r_wk[:, 0, :], r_a[:, 0, :], ACT.Exp, bias=r_negM[:, 0, P - 1:P])
                nc.scalar.activation(r_int[:, 0, :], r_negM[:, 1, :], ACT.Exp, bias=r_bM[:, 0, P - 1:P])
                nc.scalar.activation(r_emc[:], r_bM[:], ACT.Exp, scale=-1.0).then_inc(rows_act, 1)
                copy(neg[0:H, :, :], r_negM[:]).then_inc(neg_hi, 1)

            def v_turn(i):
                for n in range(2):
                    for q in range(BC):
                        c = Chunk(G_V + n * BC + q, i, 2 * BC)
                        split(c.next())
                        if starts(i) and n == 0 and q == 0:
                            act.wait_ge(setup2, 7)
                            gate_rows_1()
                        if starts(i) and n == 0 and q == 2:
                            gate_rows_2()
                    act.wait_ge(lo_used, c.count(1))
                    for r in range(RT):
                        last = copy(vx[:, r, bass.ds(i * 4 + n * 2, 2), 0:DV],
                                    ps[:, 2 * n + r, :].rearrange("p (h d) -> p h d", h=2),
                                    scale=r_x[:, 0, r:r + 1])
                    last.then_inc(act_out, 1)

            v_turn(0)
            with act.Fori(1, 2) as i:
                v_turn(i)

            def p_taken(d):
                act.wait_ge(p_turned, d + 1)
                if not starts(d):
                    act.wait_ge(cu_lo, d)
                copy(pT[:, :, 32:32 + SEQ], bank_kt(6)).then_inc(p_copied, 1)
                for k in range(KB):
                    last = copy(uT[:, k, :], bank_kt(6)[:, k, :],
                                scale=vecT[:, bass.ds(V_TAP + (TAPS - 1) * KC + k + d * KB, 1)])
                last.then_inc(p_read, 1)

            def cu_high(d):
                act.wait_ge(u_done, d + 1)
                copy(cuT_hi[:, bass.ds(d * KB, KB), :], uT[:]).then_inc(cu_hi, 1)

            def conv_turn(i):
                first = starts(i)

                def state(b):
                    act.wait_ge(first_done, i * 2 + b + 1)
                    copy(head_C[:, b, :], ps[:, 7, 0:DV + 1]).then_inc(state_out, 1)

                def carried(b):
                    act.wait_ge(second_done, i * 2 + b + 1)
                    if not (first and b == 0):
                        act.wait_ge(h1_done, i * 2 + b)
                    copy(inter[:], ps[:, 7, 0:DV + 1], scale=head_cols[:, b, INT:INT + 1]).then_inc(inter_out, 1)

                for j in range(3 * BC):
                    c = Chunk(G_CONV + j, i, 3 * BC)
                    split(c.next())
                    if j == 0 and not first:
                        p_taken(i - 1)
                    if j == 2:
                        if not first:
                            cu_high(i - 1)
                            act.wait_ge(second_done, i * 2)
                        for b in range(2):
                            act.wait_ge(turned, i * 2 + b + 1)
                            copy(head_qkT[:, b, 0:2, :], ps[:, 6 + b, 0:2 * P], scale=QK_SCALE)
                            copy(head_qkT[:, b, 2:4, :], ps[:, 6 + b, 2 * P:4 * P]).then_inc(turned_out, 1)
                    if j == 3:
                        if not first:
                            act.wait_ge(p_turned, i)
                        take(c, 0, nat[:])
                        for b in range(2):
                            act.wait_ge(weighed, i * 2 + b + 1)
                            for r in range(RT):
                                last = nc.scalar.activation(head_w[:, b, r, :], head_w[:, b, r, :], ACT.Exp,
                                                            bias=head_cols[:, b, A_IN + r:A_IN + r + 1])
                            last.then_inc(exped, 1)
                    if j == 5:
                        act.wait_ge(cb_turned, i + 1)
                        if not first:
                            act.wait_ge(u_done, i)
                        copy(cbT[:], bank_kt(6)).then_inc(cb_out, 1)
                    if j == 6:
                        state(0)
                    if j == 7:
                        take(c, 1, nat[:])
                        carried(0)
                    if j == 8:
                        state(1)
                    if j == 9:
                        carried(1)
                    if j == 10:
                        act.wait_ge(h1_done, i * 2 + 2)
                        for b in range(2):
                            for r, scratch in enumerate((head_sc, head_w)):
                                nc.scalar.activation(
                                    scratch[:, b, :, :].rearrange("p r t -> p (r t)"), vx[:, r, i * 2 + b, 0:DV],
                                    ACT.Square, accum_out=ss[:, bass.ds(r * H + b + i * 2, 1)]).then_inc(h_squared, 1)

            conv_turn(0)
            with act.Fori(1, NB) as i:
                conv_turn(i)

            for n in range(NB):
                for q in range(BC):
                    c = Chunk(G_O + n * BC + q)
                    split(c.next())
                    if n == 0:
                        if q == 0:
                            p_taken(NB - 1)
                        if q == 2:
                            cu_high(NB - 1)
                    if n > 0 and q == 1:
                        group_hi(GRP_HM + n, hmT_hi, (n - 1) * KB, 0, V_MH)
                if n > 0:
                    act.wait_ge(hm_done, n)
                else:
                    act.wait_ge(p_turned, NB)
                take(c, n % 2, nat[:], ACT.Sigmoid)

            def merge_turn(i):
                first = starts(i)
                for j in range(4 * BC):
                    c = Chunk(G_MERGE + j, i, 4 * BC)
                    split(c.next())
                    if j == 1:
                        if first:
                            group_hi(GRP_M, hmT_hi, (NB - 1) * KB, 0, V_MH)
                        else:
                            group_hi(i + GRP_M, mT_hi, (i - 1) * KB, 0)
                    if j == 3:
                        if not first:
                            act.wait_ge(dve_out, V_MERGE + i * 2)
                        take(c, 0, gate[:], ACT.Sigmoid)
                    if j == 3 + 2 * BC:
                        act.wait_ge(dve_out, V_MERGE + 1 + i * 2)
                        take(c, 0, gate[:], ACT.Sigmoid)

            merge_turn(0)
            with act.Fori(1, NB) as i:
                merge_turn(i)

            for n in range(NB):
                for q in range(BC):
                    c = Chunk(G_OUT + n * BC + q)
                    split(c.next())
                    if q == 1:
                        if n == 0:
                            group_hi(GRP_F, mT_hi, (NB - 1) * KB, 0)
                        else:
                            group_hi(GRP_F + n, fT_hi, (n - 1) * KB, 0, V_FN)
                act.wait_ge(dve_out, V_OUT + n + 1)
                for r in range(RT):
                    if n + r > 0:
                        act.wait_ge(x1_squared, n * RT + r)
                    nc.scalar.activation(prod[:, 0, :], x1[:, r, n * COLS:(n + 1) * COLS], ACT.Square,
                                         accum_out=ss1[:, r, n:n + 1]).then_inc(x1_squared, 1)

            def act_taken(d):
                act.wait_ge(act_turned, d + 1)
                copy(actT[:, bass.ds(d * KB, KB), :], bank_kt(4)).then_inc(act_out_of, 1)

            def ffn_turn(i):
                first = starts(i)
                for j in range(2 * BC):
                    c = Chunk(G_FFN + j, i, 2 * BC)
                    split(c.next())
                    if j == 1:
                        if first:
                            group_hi(GRP_F + NB, fT_hi, (NB - 1) * KB, 0, V_FN)
                        else:
                            act_taken(i - 1)
                    if j == 3:
                        act.wait_ge(lo_used, c.count(1))
                        if first:
                            act.wait_ge(x1_rstd, 1)
                        else:
                            act.wait_ge(dve_out, V_FFN + i)
                        for r in range(RT):
                            last = nc.scalar.activation(gate[:, r, :], ps[:, r, :], ACT.Silu, scale=r_x[:, 1, r:r + 1])
                        last.then_inc(act_out, 1)

            def stage(chunk):
                if not (isinstance(chunk.turn, int) and chunk.count(0) < G_DOWN + 2):
                    act.wait_ge(lo_used, chunk.count(-1))
                copy(a_hi[:, chunk.split, :], actT[:, chunk.count(-G_DOWN), :]).then_inc(a_hi_staged, 1)

            def down_turn(i, last=False):
                for n in range(RAW_SLOTS):
                    c = Chunk(G_DOWN + n, i, RAW_SLOTS)
                    if not (last and n == RAW_SLOTS - 1):
                        split(c.next())
                        if starts(i) and n == 0:
                            act_taken(FB - 1)
                        stage(c.next())

            ffn_turn(0)
            ffn_turn(1)
            act.wait_ge(act_out_of, 1)
            stage(Chunk(G_DOWN))
            with act.Fori(2, FB) as i:
                ffn_turn(i)
            down_turn(0)
            with act.Fori(1, FC // RAW_SLOTS - 1) as i:
                down_turn(i)
            down_turn(FC // RAW_SLOTS - 1, last=True)
            for r in range(RT):
                for n in range(NB):
                    act.wait_ge(y_sum, r * NB + n + 1)
                    if r > 0:
                        act.wait_ge(y_total, r)
                    nc.scalar.activation(sq_y[:, n * COLS:(n + 1) * COLS], x1[:, r, n * COLS:(n + 1) * COLS],
                                         ACT.Square, accum_out=ss1[:, r, n:n + 1]).then_inc(y_squared, 1)
                act.wait_ge(y_rstd, r + 1)
                for n in range(NB // 2):
                    act.wait_ge(y_gained, r * (NB // 2) + n + 1)
                    part = y[:, r, (NB // 2 + n) * COLS:(NB // 2 + n + 1) * COLS]
                    copy(part, part, scale=r_x[:, 0, r:r + 1]).then_inc(y_right, 1)

        @block.vector
        def _(dve):
            V = nc.vector

            def split(chunk):
                dve.wait_ge(hi_split, chunk.count(1))
                if not (isinstance(chunk.turn, int) and chunk.count(0) < SPLIT_SLOTS):
                    dve.wait_ge(lo_used, chunk.count(1 - SPLIT_SLOTS))
                V.tensor_tensor(w_lo[:, chunk.split, :], w_raw[:, chunk.raw, :],
                                w_hi[:, chunk.split, :].bitcast(F32), ALU.subtract).then_inc(lo_split, 1)

            bank_kt = lambda b0: ps[:, b0:b0 + 2, :].rearrange("p b (k t) -> p (b k) t", k=2)

            def group_lo(n, steps, dst, hi, k0, scale_at=None):
                src = bank_kt(4)
                if scale_at is None:
                    dve.wait_ge(grp_hi, steps + 1)
                    V.tensor_tensor(dst[:, bass.ds(k0, KB), :], src, hi[:, bass.ds(k0, KB), :].bitcast(F32),
                                    ALU.subtract).then_inc(grp_lo, 1)
                    return
                for k in range(KB):
                    if k % 2 == 0:
                        dve.wait_ge(grp_hi, steps + k + 2)
                    c = scale_at + k0 + k
                    last = V.scalar_tensor_tensor(out=dst[:, k0 + k, :], in0=src[:, k, :], scalar=vecT[:, c:c + 1],
                                                  in1=hi[:, k0 + k, :].bitcast(F32), op0=ALU.mult, op1=ALU.subtract)
                last.then_inc(grp_lo, 1)

            def x_low(g):
                for k in range(KB):
                    c = g * KB + k
                    if k % 2 == 0:
                        dve.wait_ge(x_hi_done, c + 2)
                    V.scalar_tensor_tensor(
                        out=xT_lo[:, c, :], in0=bank_kt(4 + 2 * (g % 2))[:, k, :],
                        scalar=vecT[:, V_MIX + c:V_MIX + c + 1], in1=xT_hi[:, c, :].bitcast(F32),
                        op0=ALU.mult, op1=ALU.subtract).then_inc(x_lo_done, 1)

            x_low(0)
            split(Chunk(G_QK))
            for q in range(BC):
                if q + 1 < NB:
                    x_low(q + 1)
                split(Chunk(G_QK + q).next())
                if q == 3:
                    dve.wait_ge(x_rstd, RT)
                    dve.wait_ge(setup, 3)
                    for r in range(RT):
                        V.tensor_scalar(out=diag[:, r, :], in0=ident[:], scalar1=r_x[:, 0, r:r + 1], scalar2=None,
                                        op0=ALU.mult).then_inc(diag_done, 1)
                    dve.wait_ge(gw_hi, 1)
                    part = lambda c: wg[:, :, c:c + 64].rearrange("p k (g c) -> p k g c", g=2)[:, :, :, 0:H]
                    V.tensor_tensor(part(64), wg_raw[:].rearrange("p k (g c) -> p k g c", g=2), part(0).bitcast(F32),
                                    ALU.subtract).then_inc(gw_lo, 1)
            with dve.Fori(1, 4) as i:
                for q in range(BC):
                    split(Chunk(G_QK + q, i, BC).next())

            def step(ins, n):
                ins.then_inc(rows_dve, 1)
                dve.wait_ge(rows_dve, n)

            def gate_rows_1():
                dve.wait_ge(gates_done, 1)
                dve.wait_ge(small_landed[2], 32)
                flat_row = lambda r: r[:].rearrange("h r t -> h (r t)")
                step(V.tensor_copy(r_row[:], ps[:, 7, 0:SEQ]), 1)
                for n, (at_row, r) in enumerate(((0, r_a), (32, r_lf), (64, r_t), (96, r_b))):
                    V.tensor_tensor(flat_row(r), ps[at_row:at_row + H, 6, 0:SEQ], r_row[at_row:at_row + H, :],
                                    ALU.mult).then_inc(rows_dve, 1)
                dve.wait_ge(rows_dve, 5)
                V.scalar_tensor_tensor(out=r_a[:], in0=r_a[:], scalar=gate_bias[:, 0:1], in1=r_t[:], op0=ALU.add,
                                       op1=ALU.add).then_inc(rows_dve, 1)
                step(V.scalar_tensor_tensor(out=r_lf[:], in0=r_lf[:], scalar=gate_bias[:, 1:2], in1=r_b[:],
                                            op0=ALU.add, op1=ALU.add), 7)
                V.scalar_tensor_tensor(out=r_t[:], in0=r_lf[:], scalar=-1.0, in1=r_lf[:], op0=ALU.mult,
                                       op1=ALU.min).then_inc(rows_dve, 1)

            def gate_rows_2():
                dve.wait_ge(rows_dve, 8)
                dve.wait_ge(rows_act, 2)
                row_ones = ones[0:H, :].bitcast(F32)
                step(V.scalar_tensor_tensor(out=r_lf[:], in0=r_lf[:], scalar=0.0, in1=r_t[:], op0=ALU.min,
                                            op1=ALU.subtract), 9)
                V.tensor_tensor_scan(r_b[:, 0, :], row_ones, r_lf[:, 0, :], 0.0, ALU.mult,
                                     ALU.add).then_inc(rows_dve, 1)
                step(V.tensor_tensor_scan(r_b[:, 1, :], row_ones, r_lf[:, 1, :], 0.0, ALU.mult, ALU.add), 11)
                step(V.tensor_tensor(r_a[:], r_a[:], r_b[:], ALU.subtract), 12)
                step(V.tensor_tensor_scan(r_M[:, 0, :], row_ones, r_a[:, 0, :], 0.0, ALU.mult, ALU.max), 13)
                step(V.tensor_tensor(r_bM[:, 0, :], r_M[:, 0, :], r_b[:, 0, :], ALU.add), 14)
                step(V.tensor_tensor_scan(r_M[:, 1, :], row_ones, r_a[:, 1, :], r_bM[:, 0, P - 1:P], ALU.mult,
                                          ALU.max), 15)
                V.tensor_tensor(r_bM[:, 1, :], r_M[:, 1, :], r_b[:, 1, :], ALU.add).then_inc(rows_dve, 1)
                V.tensor_scalar(out=r_negM[:], in0=r_M[:], scalar1=-1.0, scalar2=None,
                                op0=ALU.mult).then_inc(rows_dve, 1)

            for q in range(BC):
                split(Chunk(G_V + q).next())
                if q == 0:
                    dve.wait_ge(setup2, 7)
                    gate_rows_1()
                if q == 1:
                    gate_rows_2()
                if q == 3:
                    dve.wait_ge(neg_hi, 1)
                    V.tensor_tensor(neg[32:32 + H, :, :], r_negM[:], neg[0:H, :, :].bitcast(F32),
                                    ALU.subtract).then_inc(neg_lo, 1)
                    V.tensor_tensor(pick[:], ident[0:64, 0:H], ident[0:64, 32:32 + H], ALU.add).then_inc(neg_lo, 1)
            with dve.Fori(1, 4) as i:
                for q in range(BC):
                    split(Chunk(G_V + q, i, BC).next())
            dve.wait_ge(cols_turned, 1)
            V.tensor_copy(cols[:].rearrange("p a h -> p (a h)"), ps[:, 7, 0:6 * H]).then_inc(cols_ready, 1)

            def tap(d, j):
                for k in range(KB):
                    last = V.scalar_tensor_tensor(
                        out=uT[:, k, :], in0=pT[:, k, PAD + j:PAD + j + SEQ],
                        scalar=vecT[:, bass.ds(V_TAP + j * KC + k + d * KB, 1)], in1=uT[:, k, :],
                        op0=ALU.mult, op1=ALU.add)
                last.then_inc(tap_step, 1)

            def conv_low(d):
                dve.wait_ge(cu_hi, d + 1)
                V.tensor_tensor(cuT_lo[:, bass.ds(d * KB, KB), :], uT[:],
                                cuT_hi[:, bass.ds(d * KB, KB), :].bitcast(F32), ALU.subtract).then_inc(cu_lo, 1)

            def conv_0(d):
                dve.wait_ge(p_read, d + 1)
                tap(d, 1)

            def conv_1(d):
                dve.wait_ge(tap_step, d * 2 + 1)
                tap(d, 0)
                dve.wait_ge(tap_step, d * 2 + 2)
                dve.wait_ge(cb_out, d + 1)
                V.tensor_tensor(uT[:], uT[:], cbT[:], ALU.mult).then_inc(u_done, 1)

            def conv_turn(i):
                first = starts(i)

                def normalise(b, source, emc, dst, steps, done):
                    d = source[:, DV:DV + 1]
                    V.tensor_scalar(out=den[:, 0:1], in0=d, scalar1=head_cols[:, b, emc:emc + 1], scalar2=None,
                                    op0=ALU.max).then_inc(den_step, 1)
                    dve.wait_ge(den_step, steps + 1)
                    V.scalar_tensor_tensor(out=den[:, 1:2], in0=d, scalar=-1.0, in1=den[:, 0:1], op0=ALU.mult,
                                           op1=ALU.max).then_inc(den_step, 1)
                    dve.wait_ge(den_step, steps + 2)
                    V.reciprocal(den[:, 2:3], den[:, 1:2]).then_inc(den_step, 1)
                    dve.wait_ge(den_step, steps + 3)
                    V.tensor_scalar(out=dst, in0=source[:, 0:DV], scalar1=den[:, 2:3], scalar2=None,
                                    op0=ALU.mult).then_inc(done, 1)

                STEPS = 7

                def h_first(b):
                    dve.wait_ge(first_done, i * 2 + b + 1)
                    normalise(b, ps[:, 6, 0:DV + 1], EMC, vx[:, 0, i * 2 + b, 0:DV],
                              i * (2 * STEPS) + b * STEPS, h0_done)

                def h_second(b):
                    dve.wait_ge(inter_out, i * 2 + b + 1)
                    V.tensor_tensor(num[:], ps[:, 6, 0:DV + 1], inter[:], ALU.add).then_inc(den_step, 1)
                    dve.wait_ge(den_step, i * (2 * STEPS) + b * STEPS + 4)
                    normalise(b, num[:], EMC + 1, vx[:, 1, i * 2 + b, 0:DV],
                              i * (2 * STEPS) + b * STEPS + 4, h1_done)

                for j in range(3 * BC):
                    c = Chunk(G_CONV + j, i, 3 * BC)
                    split(c.next())
                    if j == 0 and not first:
                        conv_0(i - 1)
                    if j == 1:
                        if not first:
                            dve.wait_ge(scored, i * 2)
                        else:
                            dve.wait_ge(cols_turned, 1)
                            dve.wait_ge(neg_lo, 2)
                        for b in range(2):
                            V.tensor_scalar(out=sel[b][:], in0=neg[:].bitcast(F32),
                                            scalar1=pick[:, bass.ds(i * 2 + b, 1)],
                                            scalar2=None, op0=ALU.mult).then_inc(selected, 1)
                        if not first:
                            conv_1(i - 1)
                    if j == 2 and not first:
                        conv_low(i - 1)
                    if j == 3:
                        for b in range(2):
                            dve.wait_ge(scored, i * 2 + b + 1)
                            V.tensor_tensor(head_w[:, b, :, :], ps[:, 6 + b, 2 * P:4 * P].rearrange("p (r t) -> p r t", r=RT),
                                            causal[:].rearrange("p (o t) -> p o t", o=1).to_broadcast([P, RT, P]),
                                            ALU.add).then_inc(weighed, 1)
                        for b in range(2):
                            dve.wait_ge(exped, i * 2 + b + 1)
                            if not first:
                                dve.wait_ge(second_done, i * 2)
                            V.tensor_tensor(head_sc[:, b, :, :], ps[:, 6 + b, 0:2 * P].rearrange("p (r t) -> p r t", r=RT),
                                            head_w[:, b, :, :], ALU.mult).then_inc(scores_done, 1)
                    if j == 4:
                        for b in range(2):
                            dve.wait_ge(staged, i * 2 + b + 1)
                            V.tensor_scalar(out=head_kw[:, b, :], in0=head_qk[:, b, 2, :],
                                            scalar1=head_cols[:, b, WK:WK + 1], scalar2=None,
                                            op0=ALU.mult).then_inc(kw_done, 1)
                    if j == 6:
                        h_first(0)
                    if j == 7:
                        h_second(0)
                    if j == 8:
                        h_first(1)
                    if j == 9:
                        h_second(1)
                dve.wait_ge(lo_used, c.count(1))
                dve.wait_ge(act_out, A_CONV + 2 + i * 2)
                for r in range(RT):
                    last = V.scalar_tensor_tensor(out=nat[:, r, :], in0=ps[:, 4 + r, :], scalar=r_x[:, 0, r:r + 1],
                                                  in1=nat[:, r, :], op0=ALU.mult, op1=ALU.mult)
                last.then_inc(dve_out, 1)

            conv_turn(0)
            with dve.Fori(1, NB) as i:
                conv_turn(i)

            for n in range(NB):
                for q in range(BC):
                    c = Chunk(G_O + n * BC + q)
                    split(c.next())
                    if n == 0 and q < 3:
                        (conv_0, conv_1, conv_low)[q](NB - 1)
                    if n > 0 and q == 1:
                        group_lo(GRP_HM + n, HI_HM + (n - 1) * KB, hmT_lo, hmT_hi, (n - 1) * KB, V_MH)
                dve.wait_ge(act_out, A_O + n + 1)
                if n == 0:
                    dve.wait_ge(h_rstd, 1)
                else:
                    dve.wait_ge(grp_turned, GRP_HM + n)
                for r in range(RT):
                    for b in range(2):
                        h = 2 * n + b
                        last = V.scalar_tensor_tensor(out=hm[:, r, b * DV:(b + 1) * DV], in0=vx[:, r, h, 0:DV],
                                                      scalar=rstd[:, r * H + h:r * H + h + 1],
                                                      in1=nat[:, r, b * DV:(b + 1) * DV], op0=ALU.mult, op1=ALU.mult)
                last.then_inc(hm_done, 1)

            def merge_turn(i):
                first = starts(i)
                for j in range(4 * BC):
                    c = Chunk(G_MERGE + j, i, 4 * BC)
                    split(c.next())
                    if j == 1:
                        if first:
                            group_lo(GRP_M, HI_HM + (NB - 1) * KB, hmT_lo, hmT_hi, (NB - 1) * KB, V_MH)
                        else:
                            group_lo(i + GRP_M, HI_M - 1 + i, mT_lo, mT_hi, (i - 1) * KB)
                    if j == 3 + BC:
                        dve.wait_ge(lo_used, c.count(1))
                        dve.wait_ge(act_out, A_MERGE + 1 + i * 2)
                        V.tensor_tensor(prod[:], ps[:, 2:4, :], gate[:], ALU.mult).then_inc(dve_out, 1)
                dve.wait_ge(lo_used, c.count(1))
                dve.wait_ge(act_out, A_MERGE + 2 + i * 2)
                if not first:
                    dve.wait_ge(grp_turned, i + GRP_M)
                V.tensor_tensor(merged[:], ps[:, 2:4, :], gate[:], ALU.mult).then_inc(dve_out, 1)
                dve.wait_ge(dve_out, V_MERGE + 2 + i * 2)
                V.tensor_tensor(merged[:], merged[:], prod[:], ALU.add).then_inc(m_done, 1)

            merge_turn(0)
            with dve.Fori(1, NB) as i:
                merge_turn(i)

            for n in range(NB):
                for q in range(BC):
                    c = Chunk(G_OUT + n * BC + q)
                    split(c.next())
                    if q == 1:
                        if n == 0:
                            group_lo(GRP_F, HI_M + NB - 1, mT_lo, mT_hi, (NB - 1) * KB)
                        else:
                            group_lo(GRP_F + n, HI_F + (n - 1) * KB, fT_lo, fT_hi, (n - 1) * KB, V_FN)
                dve.wait_ge(lo_used, c.count(1))
                if n == 0:
                    dve.wait_ge(x_again, 16)
                part = x1[:, :, n * COLS:(n + 1) * COLS]
                V.tensor_tensor(part, ps[:, 2 * (n % 2):2 * (n % 2) + 2, :], part, ALU.add).then_inc(dve_out, 1)

            def ffn_turn(i):
                first = starts(i)
                for j in range(2 * BC):
                    c = Chunk(G_FFN + j, i, 2 * BC)
                    split(c.next())
                    if first and j == 0:
                        dve.wait_ge(x1_squared, RT * NB)
                        V.tensor_reduce(sums[:], ss1[:], axis=AX.X, op=ALU.add).then_inc(x1_summed, 1)
                    if first and j == 1:
                        group_lo(GRP_F + NB, HI_F + (NB - 1) * KB, fT_lo, fT_hi, (NB - 1) * KB, V_FN)
                dve.wait_ge(lo_used, c.count(1))
                dve.wait_ge(act_out, A_FFN + 1 + i)
                if not first:
                    dve.wait_ge(act_turned, i)
                for r in range(RT):
                    last = V.scalar_tensor_tensor(out=merged[:, r, :], in0=ps[:, 2 + r, :], scalar=r_x[:, 1, r:r + 1],
                                                  in1=gate[:, r, :], op0=ALU.mult, op1=ALU.mult)
                last.then_inc(dve_out, 1)

            def stage(chunk):
                dve.wait_ge(a_hi_staged, chunk.count(1 - G_DOWN))
                if not (isinstance(chunk.turn, int) and chunk.count(0) < G_DOWN + 2):
                    dve.wait_ge(lo_used, chunk.count(-1))
                V.tensor_tensor(a_lo[:, chunk.split, :], actT[:, chunk.count(-G_DOWN), :],
                                a_hi[:, chunk.split, :].bitcast(F32), ALU.subtract).then_inc(a_lo_staged, 1)

            ffn_turn(0)
            ffn_turn(1)
            stage(Chunk(G_DOWN))
            with dve.Fori(2, FB) as i:
                ffn_turn(i)

            def down_turn(i, last=False):
                for n in range(RAW_SLOTS):
                    c = Chunk(G_DOWN + n, i, RAW_SLOTS)
                    if last and n == RAW_SLOTS - 2:
                        stage(c.next())
                        split(c.next())
                    elif not (last and n == RAW_SLOTS - 1):
                        split(c.next())
                        stage(c.next())

            down_turn(0)
            with dve.Fori(1, FC // RAW_SLOTS - 1) as i:
                down_turn(i)
            down_turn(FC // RAW_SLOTS - 1, last=True)

            dve.wait_ge(final_landed, 16)
            for r in range(RT):
                block_of = lambda t, n: t[:, r, n * COLS:(n + 1) * COLS]

                def gained(n):
                    V.tensor_tensor(block_of(y, NB // 2 + n), block_of(x1, NB // 2 + n),
                                    g_final[:, (NB // 2 + n) * COLS:(NB // 2 + n + 1) * COLS],
                                    ALU.mult).then_inc(y_gained, 1)

                for n in range(NB):
                    dve.wait_ge(down_done, r * NB + n + 1)
                    V.tensor_tensor(block_of(x1, n), ps[:, 4 * r + n, :], block_of(x1, n), ALU.add).then_inc(y_sum, 1)
                dve.wait_ge(y_sum, (r + 1) * NB)
                gained(0)
                dve.wait_ge(y_squared, (r + 1) * NB)
                V.tensor_reduce(sums[:, r:r + 1], ss1[:, r, :], axis=AX.X, op=ALU.add).then_inc(y_total, 1)
                gained(1)
                dve.wait_ge(y_rstd, r + 1)
                for n in range(NB // 2):
                    V.scalar_tensor_tensor(out=block_of(y, n), in0=block_of(x1, n), scalar=r_x[:, 0, r:r + 1],
                                           in1=g_final[:, n * COLS:(n + 1) * COLS], op0=ALU.mult,
                                           op1=ALU.mult).then_inc(y_left, 1)

        @block.tensor
        def _(pe):
            T = nc.tensor

            def project(chunk, banks, hi, lo, q, midway=None):
                rows = lambda part, k, r: part[:, q * KB + k, r * P:(r + 1) * P]
                first = isinstance(chunk.turn, int) and chunk.count(0) == G_QK
                if not first:
                    pe.wait_ge(hi_split, chunk.count(1))
                for k in range(KB):
                    if first:
                        pe.wait_ge(*((half_hi, 1) if k < KB // 2 else (hi_split, 1)))
                        pe.wait_ge(x_lo_done, k + 1)
                    w = w_hi[:, chunk.split, k * COLS:(k + 1) * COLS]
                    for r in range(RT):
                        T.matmul(ps[:, banks + r, :], rows(hi, k, r), w, start=(q == 0 and k == 0), stop=False)
                        last = T.matmul(ps[:, banks + r, :], rows(lo, k, r), w, start=False, stop=False)
                    if k == 1 and midway is not None:
                        midway()
                last.then_inc(hi_used, 1)
                pe.wait_ge(lo_split, chunk.count(1))
                for k in range(KB):
                    w = w_lo[:, chunk.split, k * COLS:(k + 1) * COLS]
                    for r in range(RT):
                        last = T.matmul(ps[:, banks + r, :], rows(hi, k, r), w, start=False,
                                        stop=(q == BC - 1 and k == KB - 1))
                last.then_inc(lo_used, 1)

            def turn_block(source, bank, done, each_bank=False):
                for k in range(KB):
                    for r in range(RT):
                        at_col = (k % 2) * SEQ + r * P
                        last = T.transpose(ps[:, bank + k // 2, at_col:at_col + P],
                                           source[:, r, k * P:(k + 1) * P], ident[:])
                    if k == KB - 1 or (each_bank and k == 1):
                        last.then_inc(done, 1)

            def turn_x(g):
                pe.wait_ge(x_landed[g], 16)
                if g >= 2:
                    pe.wait_ge(x_lo_done, (g - 1) * KB)
                turn_block(xn[:, :, g * COLS:(g + 1) * COLS], 4 + 2 * (g % 2), x_turned, each_bank=True)

            def warm(times):
                for n in range(times):
                    T.transpose(ps[:, 3, 0:P], ident[:], ident[:])

            pe.wait_ge(setup, 3)
            warm(14)
            pe.wait_ge(small_landed[0], 64)
            T.transpose(ps[:, 2, 0:96], vec_rows[:], ident[0:96, 0:96]).then_inc(vec_turned, 1)
            turn_x(0)
            warm(12)

            for q in range(BC):
                if q > 0:
                    pe.wait_ge(x_lo_done, (q + 1) * KB)
                project(Chunk(G_QK + q), 0, xT_hi, xT_lo, q, midway=(lambda: turn_x(q + 1)) if q + 1 < NB else None)
            pe.wait_ge(vec_ready, 1)
            for q in range(BC):
                project(Chunk(G_QK + BC + q), 2, xT_hi, xT_lo, q)

            def two_blocks(at_chunk, i, blocks_before):
                for n in range(2):
                    pe.wait_ge(act_out, blocks_before + n - 1 + i * 2)
                    for q in range(BC):
                        project(Chunk(at_chunk + n * BC + q, i, 2 * BC), 2 * n, xT_hi, xT_lo, q)

            with pe.Fori(1, 2) as i:
                two_blocks(G_QK, i, 0)

            pe.wait_ge(gw_lo, 1)
            for k in range(KC):
                T.matmul(ps[:, 6, 0:SEQ], wg[:, k, :], xT_hi[:, k, :], start=(k == 0), stop=False)
                last = T.matmul(ps[:, 6, 0:SEQ], wg[:, k, :], xT_lo[:, k, :], start=False, stop=(k == KC - 1))
            pe.wait_ge(diag_done, RT)
            pe.wait_ge(setup2, 3)
            for r in range(RT):
                last = T.matmul(ps[:, 7, r * P:(r + 1) * P], ones_p[:], diag[:, r, :], start=True, stop=True)
            last.then_inc(gates_done, 1)

            with pe.Fori(0, 2) as i:
                two_blocks(G_V, i, A_V)

            pe.wait_ge(rows_act, 3)
            for n, r in enumerate((r_a[:, 0, :], r_a[:, 1, :], r_wk[:, 0, :], r_int[:, 0, :], r_emc[:, 0, :],
                                   r_emc[:, 1, :])):
                last = T.matmul(ps[:, 7, n * H:(n + 1) * H], r, ident[0:H, 0:H], start=True, stop=True)
            last.then_inc(cols_turned, 1)

            def conv_turn(i):
                first = starts(i)

                def head_turn(b):
                    pe.wait_ge(staged, i * 2 + b + 1)
                    for n in range(4):
                        last = T.transpose(ps[:, 6 + b, n * P:(n + 1) * P], head_qk[:, b, n, :], ident[:])
                    last.then_inc(turned, 1)

                def head_scores(b):
                    pe.wait_ge(turned_out, i * 2 + b + 1)
                    pe.wait_ge(selected, i * 2 + b + 1)
                    for r in range(RT):
                        T.matmul(ps[:, 6 + b, r * P:(r + 1) * P], head_qkT[:, b, 2 + r, :], head_qkT[:, b, r, :],
                                 start=True, stop=True)
                    T.matmul(ps[:, 6 + b, 2 * P:4 * P], ones[:], sel[b][:], start=True, stop=True).then_inc(scored, 1)

                def head_first(b):
                    pe.wait_ge(scores_done, i * 2 + b + 1)
                    pe.wait_ge(kw_done, i * 2 + b + 1)
                    v = vx[:, 0, i * 2 + b, :]
                    T.matmul(ps[:, 6, 0:DV + 1], head_sc[:, b, 0, :], v, start=True, stop=True)
                    T.matmul(ps[:, 7, 0:DV + 1], head_kw[:, b, :], v, start=True, stop=True).then_inc(first_done, 1)

                def head_second(b):
                    pe.wait_ge(state_out, i * 2 + b + 1)
                    pe.wait_ge(h0_done, i * 2 + b + 1)
                    T.matmul(ps[:, 6, 0:DV + 1], head_sc[:, b, 1, :], vx[:, 1, i * 2 + b, :], start=True, stop=True)
                    T.matmul(ps[:, 7, 0:DV + 1], head_qkT[:, b, 1, :], head_C[:, b, :], start=True,
                             stop=True).then_inc(second_done, 1)

                for j in range(3 * BC):
                    if j == 0:
                        pe.wait_ge(act_out, A_CONV - 1 + i * 2)
                    if j == BC:
                        pe.wait_ge(act_out, A_CONV + i * 2)
                    if j == 2 * BC and not first:
                        pe.wait_ge(dve_out, i)
                    project(Chunk(G_CONV + j, i, 3 * BC), 2 * (j // BC), xT_hi, xT_lo, j % BC)
                    if j == 0 and not first:
                        turn_p(i - 1)
                    if j == 2:
                        if first:
                            pe.wait_ge(cols_ready, 1)
                        else:
                            pe.wait_ge(p_read, i)
                        head_turn(0)
                        head_turn(1)
                    if j == 3:
                        head_scores(0)
                        head_scores(1)
                    if j == 5:
                        pe.wait_ge(act_out, A_CONV + 1 + i * 2)
                        pe.wait_ge(scores_done, i * 2 + 2)
                        turn_block(nat, 6, cb_turned)
                    if j == 6:
                        pe.wait_ge(cb_out, i + 1)
                        head_first(0)
                    if j == 7:
                        head_second(0)
                    if j == 8:
                        pe.wait_ge(h1_done, i * 2 + 1)
                        head_first(1)
                    if j == 9:
                        head_second(1)

            def turn_p(d):
                pe.wait_ge(dve_out, d + 1)
                pe.wait_ge(h1_done, d * 2 + 2)
                turn_block(nat, 6, p_turned)

            conv_turn(0)
            with pe.Fori(1, NB) as i:
                conv_turn(i)

            for n in range(NB):
                pe.wait_ge(act_out, A_O - 1 + n)
                for q in range(BC):
                    project(Chunk(G_O + n * BC + q), 2 * (n % 2), xT_hi, xT_lo, q)
                    if n == 0 and q == 0:
                        turn_p(NB - 1)
                    if n > 0 and q == 1:
                        pe.wait_ge(hm_done, n)
                        if n > 1:
                            pe.wait_ge(grp_lo, n - 1)
                        turn_block(hm, 4, grp_turned)

            def merge_turn(i):
                first = starts(i)
                for j in range(4 * BC):
                    q = j % BC
                    if j == 0:
                        pe.wait_ge(act_out, A_MERGE - 1 if first else A_MERGE + i * 2)
                    if j == BC:
                        if first:
                            pe.wait_ge(act_out, A_MERGE)
                        else:
                            pe.wait_ge(dve_out, V_MERGE + i * 2)
                    if j == 2 * BC:
                        pe.wait_ge(act_out, A_MERGE + 1 + i * 2)
                    if j == 3 * BC:
                        pe.wait_ge(dve_out, V_MERGE + 1 + i * 2)
                    if first and j == 2 * BC - 1:
                        pe.wait_ge(grp_lo, GRP_M)
                    if first and j == 3 * BC:
                        pe.wait_ge(cu_lo, NB)
                    hi, lo = {1: (hmT_hi, hmT_lo), 3: (cuT_hi, cuT_lo)}.get(j // BC, (xT_hi, xT_lo))
                    project(Chunk(G_MERGE + j, i, 4 * BC), 2 * (j // BC % 2), hi, lo, q)
                    if j == 1:
                        if first:
                            pe.wait_ge(hm_done, NB)
                            pe.wait_ge(grp_lo, GRP_M - 1)
                            turn_block(hm, 4, grp_turned)
                        else:
                            pe.wait_ge(m_done, i)
                            pe.wait_ge(grp_lo, GRP_M - 1 + i)
                            turn_block(merged, 4, grp_turned)

            merge_turn(0)
            with pe.Fori(1, NB) as i:
                merge_turn(i)

            for n in range(NB):
                if n == 0:
                    pe.wait_ge(act_out, A_FFN)
                else:
                    pe.wait_ge(dve_out, V_OUT + n - 1)
                for q in range(BC):
                    if n == 0 and q == BC - 1:
                        pe.wait_ge(grp_lo, GRP_F)
                    project(Chunk(G_OUT + n * BC + q), 2 * (n % 2), mT_hi, mT_lo, q)
                    if q == 1:
                        if n == 0:
                            pe.wait_ge(m_done, NB)
                            pe.wait_ge(grp_lo, GRP_F - 1)
                            turn_block(merged, 4, grp_turned)
                        else:
                            pe.wait_ge(grp_lo, GRP_F + n - 1)
                            turn_block(x1[:, :, (n - 1) * COLS:n * COLS], 4, grp_turned)

            def turn_act(d):
                pe.wait_ge(dve_out, V_FFN + 1 + d)
                if not starts(d):
                    pe.wait_ge(act_out_of, d)
                turn_block(merged, 4, act_turned)

            def ffn_turn(i, d=None):
                first = starts(i)
                for j in range(2 * BC):
                    if j == 0:
                        pe.wait_ge(*((dve_out, V_FFN - 1) if first else (act_out, A_FFN + i)))
                    if j == BC:
                        pe.wait_ge(dve_out, V_FFN + i)
                    if first and j == BC - 1:
                        pe.wait_ge(grp_lo, GRP_F + NB)
                    project(Chunk(G_FFN + j, i, 2 * BC), 2 * (j // BC), fT_hi, fT_lo, j % BC)
                    if j == 1:
                        if first:
                            pe.wait_ge(dve_out, V_FFN)
                            pe.wait_ge(grp_lo, GRP_F + NB - 1)
                            turn_block(x1[:, :, (NB - 1) * COLS:NB * COLS], 4, grp_turned)
                        else:
                            turn_act(i - 1)

            ffn_turn(0)
            ffn_turn(1)
            with pe.Fori(2, FB) as i:
                ffn_turn(i)

            def down_parts(chunk):
                h, l = a_hi[:, chunk.split, :], a_lo[:, chunk.split, :]
                tile = lambda part, r: part[:, r * P:(r + 1) * P]
                cols_of = lambda w, n: w[:, chunk.split, n * COLS:(n + 1) * COLS]

                def high(r, ns, start=False):
                    for n in ns:
                        T.matmul(ps[:, 4 * r + n, :], tile(h, r), cols_of(w_hi, n), start=start, stop=False)
                    for n in ns:
                        ins = T.matmul(ps[:, 4 * r + n, :], tile(l, r), cols_of(w_hi, n), start=False, stop=False)
                    return ins

                def low(r, ns, stop=False):
                    for n in ns:
                        ins = T.matmul(ps[:, 4 * r + n, :], tile(h, r), cols_of(w_lo, n), start=False, stop=stop)
                    return ins

                return high, low

            ALL = range(NB)

            def down(chunk):
                high, low = down_parts(chunk)
                pe.wait_ge(hi_split, chunk.count(1))
                pe.wait_ge(a_lo_staged, chunk.count(1 - G_DOWN))
                high(0, ALL)
                high(1, ALL).then_inc(hi_used, 1)
                pe.wait_ge(lo_split, chunk.count(1))
                low(0, ALL)
                low(1, ALL).then_inc(lo_used, 1)

            high, low = down_parts(Chunk(G_DOWN))
            pe.wait_ge(act_out, A_FFN + FB)
            pe.wait_ge(hi_split, G_DOWN + 1)
            pe.wait_ge(a_lo_staged, 1)
            high(0, (0, 1), start=True)
            high(1, (2, 3), start=True)
            turn_act(FB - 1)
            high(0, (2, 3), start=True)
            pe.wait_ge(lo_split, G_DOWN + 1)
            low(0, ALL)
            low(1, (2, 3))
            pe.wait_ge(act_out_of, FB)
            high(1, (0, 1), start=True).then_inc(hi_used, 1)
            low(1, (0, 1)).then_inc(lo_used, 1)
            for n in range(1, RAW_SLOTS):
                down(Chunk(G_DOWN + n))
            with pe.Fori(1, FC // RAW_SLOTS - 1) as i:
                for n in range(RAW_SLOTS):
                    down(Chunk(G_DOWN + n, i, RAW_SLOTS))
            last_turn = [Chunk(G_DOWN + n, FC // RAW_SLOTS - 1, RAW_SLOTS) for n in range(RAW_SLOTS)]
            for chunk in last_turn[:-2]:
                down(chunk)
            for r in range(RT):
                for chunk in last_turn[-2:]:
                    high, low = down_parts(chunk)
                    if r == 0:
                        pe.wait_ge(hi_split, chunk.count(1))
                        pe.wait_ge(a_lo_staged, chunk.count(1 - G_DOWN))
                    if chunk is not last_turn[-1]:
                        high(r, ALL)
                        if r == 0:
                            pe.wait_ge(lo_split, chunk.count(1))
                        low(r, ALL)
                        continue
                    for n in ALL:
                        high(r, (n,))
                        if r == 0 and n == 0:
                            pe.wait_ge(lo_split, chunk.count(1))
                        low(r, (n,), stop=True).then_inc(down_done, 1)


_INS = ["x", "norm_mix", "w_in", "b_igate", "b_fgate", "conv_w", "mh_norm", "w_branch_a", "w_branch_b",
        "w_out", "norm_ffn", "w_gate", "w_up", "w_down", "norm_final"]


def kernel(**inputs):
    import concourse.bacc as bacc
    from concourse.bass_utils import run_bass_kernel_spmd

    nc = bacc.Bacc("TRN2", target_bir_lowering=False, num_devices=1)
    arrays, args = {}, []
    for name in _INS:
        a = np.ascontiguousarray(inputs[name])
        arrays[f"in_{name}"] = a
        args.append(nc.dram_tensor(f"in_{name}", a.shape, mybir.dt.from_np(a.dtype), kind="ExternalInput").ap())
    out = nc.dram_tensor("out_y", inputs["x"].shape, F32, kind="ExternalOutput").ap()
    hybrid_block(nc, *args, out)
    r = run_bass_kernel_spmd(nc, [arrays], core_ids=[0])
    return r.results[0]["out_y"]
```
